# Optimizing a Trainium2 kernel written in Bass

```python
import jax, jax.numpy as jnp
from jax import lax
import numpy as np
import math
import jax
import jax.numpy as jnp

D_MODEL = 1024
BATCH = 1
SEQ = 256
DEPTH = 2

CHUNK = 64
EPS = 1e-6
PLE_DIM = 256
D_FF = 2816
FFN_RES = 0.5
N_EVEN = (DEPTH + 1) // 2
N_ODD = DEPTH // 2

GLA_HEADS = 4
GLA_V = D_MODEL // 2
GLA_DV = GLA_V // GLA_HEADS
GLA_QK = GLA_V // 2
GLA_DK = GLA_QK // GLA_HEADS
GLA_RANK = 16
GLA_GATE_TEMP = 16.0

LRU_WIDTH = D_MODEL // 2
LRU_BLOCKS = 8
LRU_BW = LRU_WIDTH // LRU_BLOCKS
CONV_W = 4
LRU_C = 8.0

MIX0_SPLITS = [int(c) for c in np.cumsum([GLA_QK, GLA_QK, GLA_V, GLA_V, GLA_RANK, LRU_WIDTH])]
MIX0_COLS = 2 * GLA_QK + 2 * GLA_V + GLA_RANK + 2 * LRU_WIDTH
MIX0_OUT = GLA_V + LRU_WIDTH

HG_DK = 128
HG_HEADS = D_MODEL // HG_DK
HG_DV = 128
HG_K = HG_HEADS * HG_DK
HG_V = HG_HEADS * HG_DV
MIX1_SPLITS = [HG_K, 2 * HG_K, 2 * HG_K + HG_V]
MIX1_COLS = 2 * HG_K + 2 * HG_V


def rmsnorm(x, g):
    xf = x.astype(jnp.float32)
    y = xf * lax.rsqrt(jnp.mean(xf * xf, axis=-1, keepdims=True) + EPS)
    return (y * g.astype(jnp.float32)).astype(x.dtype)

def swiglu(h, w1, w3, w2):
    return (jax.nn.silu(h @ w1) * (h @ w3)) @ w2

def chunk_end_gated_linear_attention(q, k, v, log_f):
    b, s, h, dk = q.shape
    dv = v.shape[-1]
    n = s // CHUNK

    def chunks(t):
        return jnp.moveaxis(t.astype(jnp.float32).reshape(b, n, CHUNK, h, t.shape[-1]), 1, 0)

    qc, kc, vc, lf = chunks(q), chunks(k), chunks(v), chunks(log_f)
    cum = jnp.cumsum(lf, axis=2)
    total = cum[:, :, -1]
    k_dec = kc * jnp.exp(total[:, :, None] - cum)
    g_chunk = jnp.exp(total)

    def step(state, xs):
        q_c, k_c, v_c, g_c = xs
        state = g_c[..., None] * state + jnp.einsum('bchk,bchv->bhkv', k_c, v_c)
        return state, jnp.einsum('bchk,bhkv->bchv', q_c, state)

    s0 = jnp.zeros((b, h, dk, dv), jnp.float32)
    _, o = lax.scan(step, s0, (qc, k_dec, vc, g_chunk))
    return jnp.moveaxis(o, 0, 1).reshape(b, s, h, dv).astype(v.dtype)

def causal_depthwise_conv(x, w, bias):
    s = x.shape[1]
    xp = jnp.pad(x, ((0, 0), (CONV_W - 1, 0), (0, 0)))
    out = xp[:, 0:s] * w[0]
    for j in range(1, CONV_W):
        out = out + xp[:, j:j + s] * w[j]
    return out + bias

def block_diag(x, w, bias):
    b, s, wd = x.shape
    xb = x.reshape(b, s, LRU_BLOCKS, LRU_BW)
    return jnp.einsum('bsgi,gij->bsgj', xb, w).reshape(b, s, wd) + bias

def rg_lru(x, w_a, b_a, w_x, b_x, lam):
    r = jax.nn.sigmoid(block_diag(x, w_a, b_a)).astype(jnp.float32)
    i = jax.nn.sigmoid(block_diag(x, w_x, b_x))
    log_a = LRU_C * r * jax.nn.log_sigmoid(lam.astype(jnp.float32))
    a = jnp.exp(log_a)
    u = jnp.sqrt(-jnp.expm1(2.0 * log_a)) * (i * x).astype(jnp.float32)

    def combine(left, right):
        a1, b1 = left
        a2, b2 = right
        return a1 * a2, a2 * b1 + b2

    _, hs = lax.associative_scan(combine, (a, u), axis=1)
    return hs.astype(x.dtype)

def mixer_gla_rglru(h, w_in, gla_gate_up, gla_gate_bias, gla_head_norm, conv_w, conv_b,
                    lru_wa, lru_ba, lru_wx, lru_bx, lru_lambda, w_out):
    b, s, _ = h.shape
    z = h @ w_in
    q, k, v, g, lr, xr, xg = jnp.split(z, MIX0_SPLITS, axis=-1)
    log_f = jax.nn.log_sigmoid((lr @ gla_gate_up + gla_gate_bias).astype(jnp.float32)) / GLA_GATE_TEMP
    o = chunk_end_gated_linear_attention(
        q.reshape(b, s, GLA_HEADS, GLA_DK) * (GLA_DK ** -0.5),
        k.reshape(b, s, GLA_HEADS, GLA_DK),
        v.reshape(b, s, GLA_HEADS, GLA_DV),
        log_f.reshape(b, s, GLA_HEADS, GLA_DK))
    o = rmsnorm(o, gla_head_norm).reshape(b, s, GLA_V) * jax.nn.silu(g)
    y = rg_lru(causal_depthwise_conv(xr, conv_w, conv_b), lru_wa, lru_ba, lru_wx, lru_bx, lru_lambda)
    y = y * jax.nn.gelu(xg)
    return jnp.concatenate([o, y], axis=-1) @ w_out

def mixer_hgrn2(h, w_in, lb, hg_head_norm, w_out):
    b, s, _ = h.shape
    z = h @ w_in
    q, fz, i, g = jnp.split(z, MIX1_SPLITS, axis=-1)
    lbf = lb.astype(jnp.float32)
    zf = fz.astype(jnp.float32)
    log_f = jnp.logaddexp(jnp.log(lbf), jnp.log1p(-lbf) + jax.nn.log_sigmoid(zf))
    k = (1.0 - lbf) * jax.nn.sigmoid(-zf)
    o = chunk_end_gated_linear_attention(
        jax.nn.silu(q).reshape(b, s, HG_HEADS, HG_DK),
        k.astype(h.dtype).reshape(b, s, HG_HEADS, HG_DK),
        i.reshape(b, s, HG_HEADS, HG_DV),
        log_f.reshape(b, s, HG_HEADS, HG_DK))
    o = rmsnorm(o, hg_head_norm).reshape(b, s, HG_V) * jax.nn.silu(g)
    return o @ w_out

def lower_bounds(lb_logits):
    sm = jax.nn.softmax(lb_logits.astype(jnp.float32), axis=0)
    return jnp.cumsum(sm, axis=0) - sm[0]

def half_ffn(x, g, w1, w3, w2):
    return x + FFN_RES * swiglu(rmsnorm(x, g), w1, w3, w2)

def first_inputs(seed: int = 0) -> dict:
    key = jax.random.key(seed)
    ks = iter(list(jax.random.split(key, 40)))

    def nrm(shape, scale):
        return jax.random.normal(next(ks), shape, jnp.float32) * scale

    def gain(shape):
        return 1.0 + nrm(shape, 0.05)

    a0 = jax.random.uniform(next(ks), (N_EVEN, LRU_WIDTH), jnp.float32, 0.9, 0.999)
    return {
        'x': nrm((BATCH, SEQ, D_MODEL), 1.0),
        'p': nrm((DEPTH, BATCH, SEQ, PLE_DIM), 1.0),
        'ffn_norm': gain((DEPTH, 2, D_MODEL)),
        'ffn_w1': nrm((DEPTH, 2, D_MODEL, D_FF), D_MODEL ** -0.5),
        'ffn_w3': nrm((DEPTH, 2, D_MODEL, D_FF), D_MODEL ** -0.5),
        'ffn_w2': nrm((DEPTH, 2, D_FF, D_MODEL), D_FF ** -0.5),
        'mix_norm': gain((DEPTH, D_MODEL)),
        'ple_norm': gain((DEPTH, D_MODEL)),
        'ple_proj': nrm((DEPTH, PLE_DIM, D_MODEL), PLE_DIM ** -0.5),
        'ple_gate': nrm((DEPTH, D_MODEL, D_MODEL), D_MODEL ** -0.5),
        'final_norm': gain((D_MODEL,)),
        'm0_w_in': nrm((N_EVEN, D_MODEL, MIX0_COLS), D_MODEL ** -0.5),
        'gla_gate_up': nrm((N_EVEN, GLA_RANK, GLA_QK), GLA_RANK ** -0.5),
        'gla_gate_bias': nrm((N_EVEN, GLA_QK), 0.1),
        'gla_head_norm': gain((N_EVEN, GLA_DV)),
        'lru_conv_w': nrm((N_EVEN, CONV_W, LRU_WIDTH), CONV_W ** -0.5),
        'lru_conv_b': nrm((N_EVEN, LRU_WIDTH), 0.02),
        'lru_wa': nrm((N_EVEN, LRU_BLOCKS, LRU_BW, LRU_BW), LRU_BW ** -0.5),
        'lru_ba': nrm((N_EVEN, LRU_WIDTH), 0.02),
        'lru_wx': nrm((N_EVEN, LRU_BLOCKS, LRU_BW, LRU_BW), LRU_BW ** -0.5),
        'lru_bx': nrm((N_EVEN, LRU_WIDTH), 0.02),
        'lru_lambda': jnp.log(a0) - jnp.log1p(-a0),
        'm0_w_out': nrm((N_EVEN, MIX0_OUT, D_MODEL), MIX0_OUT ** -0.5),
        'm1_w_in': nrm((N_ODD, D_MODEL, MIX1_COLS), D_MODEL ** -0.5),
        'hgrn_lb_logits': nrm((DEPTH, HG_K), 0.1),
        'hgrn_head_norm': gain((N_ODD, HG_DV)),
        'm1_w_out': nrm((N_ODD, HG_V, D_MODEL), HG_V ** -0.5),
    }

def first_block(x, p, ffn_norm, ffn_w1, ffn_w3, ffn_w2, mix_norm, ple_norm, ple_proj, ple_gate,
              final_norm, m0_w_in, gla_gate_up, gla_gate_bias, gla_head_norm, lru_conv_w,
              lru_conv_b, lru_wa, lru_ba, lru_wx, lru_bx, lru_lambda, m0_w_out, m1_w_in,
              hgrn_lb_logits, hgrn_head_norm, m1_w_out):
    lbs = lower_bounds(hgrn_lb_logits)
    for layer in range(DEPTH):
        x = half_ffn(x, ffn_norm[layer, 0], ffn_w1[layer, 0], ffn_w3[layer, 0], ffn_w2[layer, 0])
        h = rmsnorm(x, mix_norm[layer])
        if layer % 2 == 0:
            e = layer // 2
            x = x + mixer_gla_rglru(h, m0_w_in[e], gla_gate_up[e], gla_gate_bias[e], gla_head_norm[e],
                                    lru_conv_w[e], lru_conv_b[e], lru_wa[e], lru_ba[e], lru_wx[e],
                                    lru_bx[e], lru_lambda[e], m0_w_out[e])
        else:
            o = layer // 2
            x = x + mixer_hgrn2(h, m1_w_in[o], lbs[layer], hgrn_head_norm[o], m1_w_out[o])
        x = half_ffn(x, ffn_norm[layer, 1], ffn_w1[layer, 1], ffn_w3[layer, 1], ffn_w2[layer, 1])
        gate = jax.nn.sigmoid(rmsnorm(x, ple_norm[layer]) @ ple_gate[layer])
        x = x + gate * (p[layer] @ ple_proj[layer])
    return rmsnorm(x, final_norm)


GRID_W = 64
CTX_LEN = 256
ATTN_BLOCK = 128
ROPE_BASE = 10000.0
RMS_EPS = 1e-6

DIFF_HEADS = 4
DIFF_HEAD_DIM = 64
NA_HEADS = 8
NA_HEAD_DIM = 64
NA_WIN_ROWS_MAX = 8
NA_WIN_COLS = 16
MLA_HEADS = 8
MLA_Q_RANK = 256
MLA_KV_RANK = 128
MLA_NOPE_DIM = 64
MLA_ROPE_DIM = 32
MLA_V_DIM = 64
RET_HEADS = 4
RET_QK_DIM = 64
RET_V_DIM = 128
RET_CHUNK = 128
N_EXPERTS = 16
EC_CAPACITY_FACTOR = 2
EXPERT_FF = 1024

DIFF_WIDTH = DIFF_HEADS * 2 * DIFF_HEAD_DIM
NA_WIDTH = NA_HEADS * NA_HEAD_DIM
EVEN_IN = 3 * DIFF_WIDTH + 3 * NA_WIDTH
EVEN_OUT = DIFF_WIDTH + NA_WIDTH
MLA_QK_DIM = MLA_NOPE_DIM + MLA_ROPE_DIM
MLA_WIDTH = MLA_HEADS * MLA_V_DIM
RET_QK_WIDTH = RET_HEADS * RET_QK_DIM
RET_V_WIDTH = RET_HEADS * RET_V_DIM
ODD_IN = MLA_Q_RANK + MLA_KV_RANK + MLA_ROPE_DIM + 2 * RET_QK_WIDTH + 2 * RET_V_WIDTH
ODD_OUT = MLA_WIDTH + RET_V_WIDTH
N_EVEN_2 = (DEPTH + 1) // 2
N_ODD_2 = DEPTH // 2


def rms_norm(x, gain=None):
    xf = x.astype(jnp.float32)
    y = xf * lax.rsqrt(jnp.mean(xf * xf, axis=-1, keepdims=True) + RMS_EPS)
    if gain is not None:
        y = y * gain.astype(jnp.float32)
    return y.astype(x.dtype)

def split_cols(p, widths):
    idx, acc = [], 0
    for w in widths[:-1]:
        acc += w
        idx.append(acc)
    return jnp.split(p, idx, axis=-1)

def axial_angles(n_tokens, rot_dim):
    t = jnp.arange(n_tokens)
    rows = (t // GRID_W).astype(jnp.float32)
    cols = (t % GRID_W).astype(jnp.float32)
    m = rot_dim // 4
    freqs = ROPE_BASE ** (-jnp.arange(m, dtype=jnp.float32) / m)
    return rows[:, None] * freqs, cols[:, None] * freqs

def rope_half(x, ang):
    a, b = jnp.split(x, 2, axis=-1)
    cos = jnp.cos(ang).astype(x.dtype)
    sin = jnp.sin(ang).astype(x.dtype)
    return jnp.concatenate([a * cos - b * sin, b * cos + a * sin], axis=-1)

def apply_axial_rope(x, ang_r, ang_c):
    shape = ang_r.shape[:1] + (1,) * (x.ndim - 3) + ang_r.shape[1:]
    xr, xc = jnp.split(x, 2, axis=-1)
    return jnp.concatenate([rope_half(xr, ang_r.reshape(shape)), rope_half(xc, ang_c.reshape(shape))], axis=-1)

def sweep_query_blocks(fn, queries):
    B, L = queries[0].shape[:2]
    nb = L // ATTN_BLOCK
    blocks = tuple(jnp.moveaxis(q.reshape((B, nb, ATTN_BLOCK) + q.shape[2:]), 1, 0) for q in queries)
    out = jnp.moveaxis(lax.map(fn, blocks), 0, 1)
    return out.reshape((B, L) + out.shape[3:])

def softmax_attention(q, k, v, q_rope=None, k_rope=None):
    d = q.shape[-1] + (0 if q_rope is None else q_rope.shape[-1])
    scale = d ** -0.5

    def block(qs):
        s = jnp.einsum('bqhd,bkhd->bhqk', qs[0], k).astype(jnp.float32)
        if q_rope is not None:
            s = s + jnp.einsum('bqhr,bkr->bhqk', qs[1], k_rope).astype(jnp.float32)
        p = jax.nn.softmax(s * scale, axis=-1).astype(v.dtype)
        return jnp.einsum('bhqk,bkhe->bqhe', p, v)

    queries = (q,) if q_rope is None else (q, q_rope)
    return sweep_query_blocks(block, queries)

def diff_attention(q, k, v, lam):
    scale = DIFF_HEAD_DIM ** -0.5

    def block(qs):
        s = jnp.einsum('bqhcd,bkhcd->bhcqk', qs[0], k).astype(jnp.float32) * scale
        p = jax.nn.softmax(s, axis=-1)
        a = p[:, :, 0] - lam * p[:, :, 1]
        return jnp.einsum('bhqk,bkhe->bqhe', a.astype(v.dtype), v)

    return sweep_query_blocks(block, (q,))

def neighbourhood_attention(q, k, v, k_ctx, v_ctx, rpb):
    B, L, H, d = q.shape
    rows = L // GRID_W
    wr = min(NA_WIN_ROWS_MAX, rows)
    wc = NA_WIN_COLS
    scale = d ** -0.5
    qg = q.reshape(B, rows, GRID_W, H, d)
    kg = k.reshape(B, rows, GRID_W, H, d)
    vg = v.reshape(B, rows, GRID_W, H, d)
    cols = jnp.arange(GRID_W)
    col_start = jnp.clip(cols - wc // 2, 0, GRID_W - wc)
    col_idx = col_start[:, None] + jnp.arange(wc)[None, :]
    col_bias = rpb[:, :, col_idx - cols[:, None] + (NA_WIN_COLS - 1)]

    def row_block(r):
        rs = jnp.clip(r - wr // 2, 0, rows - wr)
        q_row = lax.dynamic_index_in_dim(qg, r, axis=1, keepdims=False)
        k_win = lax.dynamic_slice_in_dim(kg, rs, wr, axis=1)[:, :, col_idx]
        v_win = lax.dynamic_slice_in_dim(vg, rs, wr, axis=1)[:, :, col_idx]
        row_off = rs + jnp.arange(wr) - r + (NA_WIN_ROWS_MAX - 1)
        bias = jnp.transpose(jnp.take(col_bias, row_off, axis=1), (0, 2, 1, 3))
        s_loc = jnp.einsum('bqhd,brqwhd->bhqrw', q_row, k_win).astype(jnp.float32) * scale + bias[None].astype(jnp.float32)
        s_ctx = jnp.einsum('bqhd,bkhd->bhqk', q_row, k_ctx).astype(jnp.float32) * scale
        s = jnp.concatenate([s_loc.reshape(B, H, GRID_W, wr * wc), s_ctx], axis=-1)
        p = jax.nn.softmax(s, axis=-1).astype(v.dtype)
        p_loc = p[..., :wr * wc].reshape(B, H, GRID_W, wr, wc)
        p_ctx = p[..., wr * wc:]
        return jnp.einsum('bhqrw,brqwhd->bqhd', p_loc, v_win) + jnp.einsum('bhqk,bkhd->bqhd', p_ctx, v_ctx)

    out = lax.map(row_block, jnp.arange(rows))
    return jnp.moveaxis(out, 0, 1).reshape(B, L, H, d)

def retention_chunkwise(q, k, v, log_gamma, s0, include_diag):
    B, H, L, _ = q.shape
    dv = v.shape[-1]
    C = RET_CHUNK
    n = L // C
    pos = jnp.arange(C, dtype=jnp.float32)
    rel = pos[:, None] - pos[None, :]
    mask = (rel >= 0) if include_diag else (rel > 0)
    decay_in = jnp.where(mask, jnp.exp(log_gamma[:, None, None] * jnp.where(mask, rel, 0.0)), 0.0)
    decay_q = jnp.exp(log_gamma[:, None] * (pos + 1.0))[..., None]
    decay_k = jnp.exp(log_gamma[:, None] * (C - 1.0 - pos))[..., None]
    decay_chunk = jnp.exp(log_gamma * C)[:, None, None]

    def to_chunks(t):
        return jnp.moveaxis(t.reshape(B, H, n, C, t.shape[-1]), 2, 0)

    def step(state, blk):
        qb, kb, vb = blk
        inner = jnp.einsum('bhij,bhjv->bhiv', jnp.einsum('bhid,bhjd->bhij', qb, kb) * decay_in, vb)
        cross = jnp.einsum('bhid,bhdv->bhiv', qb * decay_q, state)
        new_state = decay_chunk * state + jnp.einsum('bhjd,bhjv->bhdv', kb * decay_k, vb)
        return new_state, inner + cross

    _, out = lax.scan(step, s0, (to_chunks(q), to_chunks(k), to_chunks(v)))
    return jnp.moveaxis(out, 0, 2).reshape(B, H, L, dv)

def retention_final_state(k, v, log_gamma):
    L = k.shape[2]
    w = jnp.exp(log_gamma[:, None] * (L - 1.0 - jnp.arange(L, dtype=jnp.float32)))
    return jnp.einsum('hl,bhld,bhlv->bhdv', w, k, v)

def retention_bidir(q, k, v, q_c, k_c, v_c, decay_logit, need_ctx):
    def to_bhld(t):
        return jnp.moveaxis(t, 2, 1).astype(jnp.float32)

    def flip(t):
        return jnp.flip(t, axis=2)

    kscale = RET_QK_DIM ** -0.5
    q, v, q_c, v_c = to_bhld(q), to_bhld(v), to_bhld(q_c), to_bhld(v_c)
    k, k_c = to_bhld(k) * kscale, to_bhld(k_c) * kscale
    log_g = jax.nn.log_sigmoid(decay_logit.astype(jnp.float32))
    lg_f, lg_b = log_g[0], log_g[1]
    s_f = retention_final_state(k_c, v_c, lg_f)
    s_b = retention_final_state(flip(k_c), flip(v_c), lg_b)
    out = retention_chunkwise(q, k, v, lg_f, s_f, True) + flip(retention_chunkwise(flip(q), flip(k), flip(v), lg_b, s_b, False))
    out = jnp.moveaxis(out, 1, 2)
    if not need_ctx:
        return out, None
    zero = jnp.zeros_like(s_f)
    out_c = retention_chunkwise(q_c, k_c, v_c, lg_f, zero, True) + flip(retention_chunkwise(flip(q_c), flip(k_c), flip(v_c), lg_b, zero, False))
    return out, jnp.moveaxis(out_c, 1, 2)

def even_layer(h, hc, w_in, w_out, lam_params, subln, rpb, layer_idx, need_ctx):
    B, L, _ = h.shape
    Lc = hc.shape[1]
    widths = (DIFF_WIDTH,) * 3 + (NA_WIDTH,) * 3
    aq, ak, av, nq, nk, nv = split_cols(h @ w_in, widths)
    aqc, akc, avc, nqc, nkc, nvc = split_cols(hc @ w_in, widths)

    def dh(t):
        return t.reshape(t.shape[:2] + (DIFF_HEADS, 2, DIFF_HEAD_DIM))

    def dvh(t):
        return t.reshape(t.shape[:2] + (DIFF_HEADS, 2 * DIFF_HEAD_DIM))

    def nh(t):
        return t.reshape(t.shape[:2] + (NA_HEADS, NA_HEAD_DIM))

    ang_r, ang_c = axial_angles(L, DIFF_HEAD_DIM)
    lam_init = 0.8 - 0.6 * math.exp(-0.3 * layer_idx)
    lq1, lk1, lq2, lk2 = lam_params
    lam = jnp.exp(jnp.sum(lq1 * lk1)) - jnp.exp(jnp.sum(lq2 * lk2)) + lam_init

    k_all = jnp.concatenate([apply_axial_rope(dh(ak), ang_r, ang_c), dh(akc)], axis=1)
    v_all = jnp.concatenate([dvh(av), dvh(avc)], axis=1)
    a = diff_attention(apply_axial_rope(dh(aq), ang_r, ang_c), k_all, v_all, lam)
    a = (rms_norm(a, subln) * (1.0 - lam_init)).reshape(B, L, DIFF_WIDTH)
    nb = neighbourhood_attention(nh(nq), nh(nk), nh(nv), nh(nkc), nh(nvc), rpb).reshape(B, L, NA_WIDTH)
    y = jnp.concatenate([a, nb], axis=-1) @ w_out
    if not need_ctx:
        return y, None
    ac = diff_attention(dh(aqc), dh(akc), dvh(avc), lam)
    ac = (rms_norm(ac, subln) * (1.0 - lam_init)).reshape(B, Lc, DIFF_WIDTH)
    nc = softmax_attention(nh(nqc), nh(nkc), nh(nvc)).reshape(B, Lc, NA_WIDTH)
    yc = jnp.concatenate([ac, nc], axis=-1) @ w_out
    return y, yc

def odd_layer(h, hc, w_in, w_out, q_norm, w_uq, kv_norm, w_ukv, decay_logit, need_ctx):
    B, L, _ = h.shape
    Lc = hc.shape[1]
    widths = (MLA_Q_RANK, MLA_KV_RANK, MLA_ROPE_DIM, RET_QK_WIDTH, RET_QK_WIDTH, RET_V_WIDTH, RET_V_WIDTH)
    cq, ckv, kr, rq, rk, rv, rg = split_cols(h @ w_in, widths)
    cqc, ckvc, krc, rqc, rkc, rvc, rgc = split_cols(hc @ w_in, widths)

    def mla_up(cq_, ckv_):
        n = cq_.shape[:2]
        qh = (rms_norm(cq_, q_norm) @ w_uq).reshape(n + (MLA_HEADS, MLA_QK_DIM))
        kvh = (rms_norm(ckv_, kv_norm) @ w_ukv).reshape(n + (MLA_HEADS, MLA_NOPE_DIM + MLA_V_DIM))
        return qh[..., :MLA_NOPE_DIM], qh[..., MLA_NOPE_DIM:], kvh[..., :MLA_NOPE_DIM], kvh[..., MLA_NOPE_DIM:]

    def rh(t, d):
        return t.reshape(t.shape[:2] + (RET_HEADS, d))

    qn, qr, kn, vm = mla_up(cq, ckv)
    qnc, qrc, knc, vmc = mla_up(cqc, ckvc)
    ang_r, ang_c = axial_angles(L, MLA_ROPE_DIM)
    k_rope_all = jnp.concatenate([apply_axial_rope(kr, ang_r, ang_c), krc], axis=1)
    m = softmax_attention(qn, jnp.concatenate([kn, knc], axis=1), jnp.concatenate([vm, vmc], axis=1),
                          apply_axial_rope(qr, ang_r, ang_c), k_rope_all).reshape(B, L, MLA_WIDTH)
    r, r_c = retention_bidir(rh(rq, RET_QK_DIM), rh(rk, RET_QK_DIM), rh(rv, RET_V_DIM),
                             rh(rqc, RET_QK_DIM), rh(rkc, RET_QK_DIM), rh(rvc, RET_V_DIM), decay_logit, need_ctx)
    r = rms_norm(r.astype(h.dtype)).reshape(B, L, RET_V_WIDTH) * jax.nn.silu(rg)
    y = jnp.concatenate([m, r], axis=-1) @ w_out
    if not need_ctx:
        return y, None
    mc = softmax_attention(qnc, knc, vmc, qrc, krc).reshape(B, Lc, MLA_WIDTH)
    rc = rms_norm(r_c.astype(hc.dtype)).reshape(B, Lc, RET_V_WIDTH) * jax.nn.silu(rgc)
    yc = jnp.concatenate([mc, rc], axis=-1) @ w_out
    return y, yc

def expert_choice_ffn(h, w_router, w1, w3, w2):
    B, T, _ = h.shape
    cap = (EC_CAPACITY_FACTOR * T) // N_EXPERTS
    aff = jax.nn.softmax((h @ w_router).astype(jnp.float32), axis=-1)
    gate, idx = lax.top_k(jnp.swapaxes(aff, 1, 2), cap)
    bidx = jnp.arange(B)[:, None, None]
    xe = h[bidx, idx]
    hid = jax.nn.silu(jnp.einsum('becd,edf->becf', xe, w1)) * jnp.einsum('becd,edf->becf', xe, w3)
    ye = jnp.einsum('becf,efd->becd', hid, w2) * gate[..., None].astype(h.dtype)
    return jnp.zeros_like(h).at[bidx, idx].add(ye)

def second_inputs(seed: int = 0) -> dict:
    key = jax.random.key(seed)
    ks = jax.random.split(key, 25)
    f32 = jnp.float32

    def nrm(k, shape, scale):
        return jax.random.normal(k, shape, f32) * scale

    def gain(k, shape):
        return 1.0 + 0.02 * jax.random.normal(k, shape, f32)

    decay_init = jnp.log(2.0 ** (5.0 + jnp.arange(RET_HEADS, dtype=f32)) - 1.0)
    return {
        'x': nrm(ks[0], (BATCH, SEQ, D_MODEL), 1.0),
        'c': nrm(ks[1], (BATCH, D_MODEL), 1.0),
        'ctx': nrm(ks[2], (BATCH, CTX_LEN, D_MODEL), 1.0),
        'c_ctx': nrm(ks[3], (D_MODEL,), 1.0),
        'ada_w': nrm(ks[4], (DEPTH, D_MODEL, 6 * D_MODEL), 0.5 * D_MODEL ** -0.5),
        'ada_b': nrm(ks[5], (DEPTH, 6 * D_MODEL), 0.01),
        'norm_mix': gain(ks[6], (DEPTH, D_MODEL)),
        'norm_ffn': gain(ks[7], (DEPTH, D_MODEL)),
        'final_norm': gain(ks[8], (D_MODEL,)),
        'even_w_in': nrm(ks[9], (N_EVEN_2, D_MODEL, EVEN_IN), D_MODEL ** -0.5),
        'even_w_out': nrm(ks[10], (N_EVEN_2, EVEN_OUT, D_MODEL), EVEN_OUT ** -0.5),
        'diff_lambda': nrm(ks[11], (N_EVEN_2, 4, DIFF_HEAD_DIM), 0.1),
        'diff_subln': gain(ks[12], (N_EVEN_2, 2 * DIFF_HEAD_DIM)),
        'na_rpb': nrm(ks[13], (N_EVEN_2, NA_HEADS, 2 * NA_WIN_ROWS_MAX - 1, 2 * NA_WIN_COLS - 1), 0.02),
        'odd_w_in': nrm(ks[14], (N_ODD_2, D_MODEL, ODD_IN), D_MODEL ** -0.5),
        'odd_w_out': nrm(ks[15], (N_ODD_2, ODD_OUT, D_MODEL), ODD_OUT ** -0.5),
        'mla_q_norm': gain(ks[16], (N_ODD_2, MLA_Q_RANK)),
        'mla_w_uq': nrm(ks[17], (N_ODD_2, MLA_Q_RANK, MLA_HEADS * MLA_QK_DIM), MLA_Q_RANK ** -0.5),
        'mla_kv_norm': gain(ks[18], (N_ODD_2, MLA_KV_RANK)),
        'mla_w_ukv': nrm(ks[19], (N_ODD_2, MLA_KV_RANK, MLA_HEADS * (MLA_NOPE_DIM + MLA_V_DIM)), MLA_KV_RANK ** -0.5),
        'ret_decay_logit': jnp.broadcast_to(decay_init, (N_ODD_2, 2, RET_HEADS)) + nrm(ks[20], (N_ODD_2, 2, RET_HEADS), 0.05),
        'moe_router': nrm(ks[21], (DEPTH, D_MODEL, N_EXPERTS), D_MODEL ** -0.5),
        'moe_w1': nrm(ks[22], (DEPTH, N_EXPERTS, D_MODEL, EXPERT_FF), D_MODEL ** -0.5),
        'moe_w3': nrm(ks[23], (DEPTH, N_EXPERTS, D_MODEL, EXPERT_FF), D_MODEL ** -0.5),
        'moe_w2': nrm(ks[24], (DEPTH, N_EXPERTS, EXPERT_FF, D_MODEL), EXPERT_FF ** -0.5),
    }

def second_block(x, c, ctx, c_ctx, ada_w, ada_b, norm_mix, norm_ffn, final_norm, even_w_in, even_w_out,
              diff_lambda, diff_subln, na_rpb, odd_w_in, odd_w_out, mla_q_norm, mla_w_uq, mla_kv_norm,
              mla_w_ukv, ret_decay_logit, moe_router, moe_w1, moe_w3, moe_w2):
    xc = ctx
    silu_c = jax.nn.silu(c)
    silu_cc = jax.nn.silu(c_ctx)
    for l in range(DEPTH):
        need_ctx = l < DEPTH - 1
        mods = jnp.split(silu_c @ ada_w[l] + ada_b[l], 6, axis=-1)
        sh1, sc1, g1, sh2, sc2, g2 = [m[:, None, :] for m in mods]
        sh1c, sc1c, g1c, sh2c, sc2c, g2c = jnp.split(silu_cc @ ada_w[l] + ada_b[l], 6, axis=-1)
        h = rms_norm(x, norm_mix[l]) * (1.0 + sc1) + sh1
        hc = rms_norm(xc, norm_mix[l]) * (1.0 + sc1c) + sh1c
        i = l // 2
        if l % 2 == 0:
            y, yc = even_layer(h, hc, even_w_in[i], even_w_out[i], diff_lambda[i], diff_subln[i], na_rpb[i], l, need_ctx)
        else:
            y, yc = odd_layer(h, hc, odd_w_in[i], odd_w_out[i], mla_q_norm[i], mla_w_uq[i], mla_kv_norm[i],
                              mla_w_ukv[i], ret_decay_logit[i], need_ctx)
        x = x + g1 * y
        h2 = rms_norm(x, norm_ffn[l]) * (1.0 + sc2) + sh2
        x = x + g2 * expert_choice_ffn(h2, moe_router[l], moe_w1[l], moe_w3[l], moe_w2[l])
        if need_ctx:
            xc = xc + g1c * yc
            hc2 = rms_norm(xc, norm_ffn[l]) * (1.0 + sc2c) + sh2c
            xc = xc + g2c * expert_choice_ffn(hc2, moe_router[l], moe_w1[l], moe_w3[l], moe_w2[l])
    return rms_norm(x, final_norm)


def setup_inputs(seed=0):
    out = dict(first_inputs(seed))
    for name, value in second_inputs(seed + 1).items():
        if name != "x":
            out[name + "_2"] = value
    return out


def reference(
    x, p, ffn_norm, ffn_w1, ffn_w3, ffn_w2, mix_norm, ple_norm, ple_proj, ple_gate, final_norm,
    m0_w_in, gla_gate_up, gla_gate_bias, gla_head_norm, lru_conv_w, lru_conv_b, lru_wa, lru_ba,
    lru_wx, lru_bx, lru_lambda, m0_w_out, m1_w_in, hgrn_lb_logits, hgrn_head_norm, m1_w_out,
    c_2, ctx_2, c_ctx_2, ada_w_2, ada_b_2, norm_mix_2, norm_ffn_2, final_norm_2, even_w_in_2,
    even_w_out_2, diff_lambda_2, diff_subln_2, na_rpb_2, odd_w_in_2, odd_w_out_2, mla_q_norm_2,
    mla_w_uq_2, mla_kv_norm_2, mla_w_ukv_2, ret_decay_logit_2, moe_router_2, moe_w1_2, moe_w3_2,
    moe_w2_2,
):
    x = first_block(
        x, p, ffn_norm, ffn_w1, ffn_w3, ffn_w2, mix_norm, ple_norm, ple_proj, ple_gate,
        final_norm, m0_w_in, gla_gate_up, gla_gate_bias, gla_head_norm, lru_conv_w, lru_conv_b,
        lru_wa, lru_ba, lru_wx, lru_bx, lru_lambda, m0_w_out, m1_w_in, hgrn_lb_logits,
        hgrn_head_norm, m1_w_out,
    )
    return second_block(
        x, c_2, ctx_2, c_ctx_2, ada_w_2, ada_b_2, norm_mix_2, norm_ffn_2, final_norm_2,
        even_w_in_2, even_w_out_2, diff_lambda_2, diff_subln_2, na_rpb_2, odd_w_in_2,
        odd_w_out_2, mla_q_norm_2, mla_w_uq_2, mla_kv_norm_2, mla_w_ukv_2, ret_decay_logit_2,
        moe_router_2, moe_w1_2, moe_w3_2, moe_w2_2,
    )


_drawn_inputs = setup_inputs


def setup_inputs(seed=0):
    import zlib

    import numpy as np

    out = dict(_drawn_inputs(seed))
    spreads = {}
    factors = {'ple_norm': 4.208,
     'gla_gate_bias': 3.068,
     'gla_head_norm': 2.676,
     'lru_conv_b': 2.947,
     'lru_ba': 8.0,
     'lru_bx': 8.0,
     'hgrn_lb_logits': 8.0,
     'ada_b_2': 3.906,
     'norm_mix_2': 6.853,
     'norm_ffn_2': 5.949,
     'final_norm_2': 2.709,
     'diff_lambda_2': 4.459,
     'diff_subln_2': 8.0,
     'na_rpb_2': 8.0,
     'mla_q_norm_2': 8.0,
     'mla_kv_norm_2': 8.0}
    for name, (base, spread) in spreads.items():
        noise = np.random.default_rng([zlib.crc32(name.encode()), seed]).standard_normal(out[name].shape)
        drawn = base * np.exp(spread * noise) if base else spread * noise
        out[name] = jnp.asarray(drawn.astype(out[name].dtype))
    for name, factor in factors.items():
        out[name] = (out[name] * factor).astype(out[name].dtype)
    return out
```

```python
from contextlib import ExitStack

import numpy as np

import concourse.bass as bass
from concourse import mybir

F32 = mybir.dt.float32
U32 = mybir.dt.uint32
ALU = mybir.AluOpType
ACT = mybir.ActivationFunctionType
AX_X = mybir.AxisListType.X

P = 128
D = 1024
KT = D // P
S = 256
CH = 64
NCH = S // CH
FF = 2816
FSTEPS = FF // 256
NE = 16
CAP = 2 * S // NE
EPS = 1e-6
LAM_INIT = 0.2
NEG = -1e30
GRID = 64
ROWS = S // GRID
RING = 12
SLOT = 2048

VEC_A = [("ffn_norm", 32), ("mix_norm", 16), ("ple_norm", 16), ("final_norm", 8), ("lru_conv_b", 4),
         ("lru_conv_w", 16), ("lru_ba", 4), ("lru_bx", 4), ("lru_lambda", 4), ("gla_gate_bias", 2),
         ("gla_head_norm", 1), ("hgrn_head_norm", 1), ("hgrn_lb_logits", 16)]
VEC_B = [("norm_mix_2", 16), ("norm_ffn_2", 16), ("final_norm_2", 8), ("c_2", 8), ("c_ctx_2", 8),
         ("diff_subln_2", 1), ("mla_q_norm_2", 2), ("mla_kv_norm_2", 1)]
VEC_C = [("ada_b_2", 96)]


def column_table():
    at, n, groups = {}, 0, []
    for vecs in (VEC_A, VEC_B, VEC_C):
        start = n
        for name, rows in vecs:
            at[name] = n
            n += rows
        groups.append((vecs, start, n - start))
    return at, n, groups


COL, NCOL, VEC_GROUPS = column_table()

CONST = {}
_n = 0
for _name, _w in (("ident", 128), ("ones", 128), ("sel2", 64), ("sel4", 32), ("iota_p", 4), ("reset", S), ("eps", 1)):
    CONST[_name] = (_n, _w)
    _n += _w
NCONST = _n
LATE = {}
_n = 0
for _name, _w in (("rot_d", 128), ("cos_d", S), ("sin_d", S), ("rot_m", 128), ("cos_m", S), ("sin_m", S),
                  ("iota_f", 2 * S), ("dist_f", 4 * S), ("dist_b", 4 * S)):
    LATE[_name] = (_n, _w)
    _n += _w
NLATE = _n


def constant_tables():
    c = np.zeros((P, NCONST), np.float32)
    late = np.zeros((P, NLATE), np.float32)

    def put(table, where, name, value):
        o, w = where[name]
        table[:value.shape[0], o:o + value.shape[1]] = value

    p = np.arange(P)
    put(c, CONST, "ident", np.eye(P, dtype=np.float32))
    put(c, CONST, "ones", np.ones((P, P), np.float32))
    put(c, CONST, "sel2", (p[:, None] % 64 == np.arange(64)).astype(np.float32))
    put(c, CONST, "sel4", (p[:, None] % 32 == np.arange(32)).astype(np.float32))
    put(c, CONST, "iota_p", (p[:, None] + P * np.arange(4) % (2 * P)).astype(np.float32))
    t = np.arange(S)
    put(c, CONST, "reset", np.tile((t % CH != 0).astype(np.float32), (P, 1)))

    put(c, CONST, "eps", np.full((P, 1), EPS, np.float32))

    def rotary(width, lead, total):
        rot = np.zeros((total, total), np.float32)
        cos, sin = np.ones((total, S), np.float32), np.zeros((total, S), np.float32)
        m = width // 4
        freqs = 10000.0 ** (-np.arange(m, dtype=np.float32) / m)
        for base in range(lead, total, width):
            for half, pos in ((0, t // GRID), (1, t % GRID)):
                ang = (pos.astype(np.float32)[:, None] * freqs.astype(np.float32)).astype(np.float32)
                for j in range(m):
                    a = base + half * 2 * m + j
                    b = a + m
                    rot[b, a] = -1.0
                    rot[a, b] = 1.0
                    cos[a] = cos[b] = np.cos(ang[:, j])
                    sin[a] = sin[b] = np.sin(ang[:, j])
        return rot, cos, sin

    rot, cos, sin = rotary(64, 0, 128)
    put(late, LATE, "rot_d", rot)
    put(late, LATE, "cos_d", cos)
    put(late, LATE, "sin_d", sin)
    rot, cos, sin = rotary(32, 64, 96)
    put(late, LATE, "rot_m", rot)
    put(late, LATE, "cos_m", cos)
    put(late, LATE, "sin_m", sin)
    put(late, LATE, "iota_f", np.tile(np.arange(2 * S, dtype=np.float32), (P, 1)))
    q = np.arange(S)[None, :]
    fwd, bwd = [], []
    for kt in range(2):
        key = kt * P + p[:, None]
        fwd.append(np.maximum(q - key, 0))
        bwd.append(np.maximum(key - q, 0))
    for kt in range(2):
        key = kt * P + p[:, None]
        fwd.append(q + S - key)
        bwd.append(S - q + key)
    put(late, LATE, "dist_f", np.concatenate(fwd, 1).astype(np.float32))
    put(late, LATE, "dist_b", np.concatenate(bwd, 1).astype(np.float32))
    hot = np.zeros((32, GRID, GRID), np.float32)
    for qc in range(GRID):
        start = min(max(qc - 8, 0), GRID - 16)
        hot[31, qc, :] = NEG
        for kc in range(start, start + 16):
            hot[kc - qc + 15, qc, kc] = 1.0
            hot[31, qc, kc] = 0.0
    return c, late, hot.reshape(32, GRID * GRID)


class Ring:

    def __init__(self):
        self.k, self.uses, self.i = 0, [0] * RING, None

    def next(self):
        s = self.k % RING
        self.k += 1
        n = self.uses[s]
        self.uses[s] += 1
        return s, (n if self.i is None else n + self.i)

    def loop(self, i):
        self.i = i

    def end(self, rounds):
        self.i = None
        self.uses = [u + rounds - 1 for u in self.uses]


def two_blocks(nc, T, out):
    with ExitStack() as ctx:
        def sb(name, shape, dt=F32):
            return ctx.enter_context(nc.sbuf_tensor(name, shape, dt))

        def sem(name):
            return ctx.enter_context(nc.semaphore(name))

        ring = sb("ring", [P, RING, SLOT])
        XC = sb("XC", [P, KT, 2 * S])
        H = sb("H", [P, KT, 2 * S])
        AR = sb("AR", [P, 19328])
        col = sb("col", [P, NCOL])
        cst = sb("cst", [P, NCONST])
        MODS = sb("MODS", [P, 2, 48, 2])
        bank = [ctx.enter_context(nc.psum_tensor(f"bank{i}", [P, 512], F32)) for i in range(8)]

        def const(name):
            o, w = CONST[name]
            return cst[:, o:o + w]

        def area(at, *dims):
            n = int(np.prod(dims))
            assert at + n <= 19328
            v = AR[:, at:at + n]
            if len(dims) == 2:
                v = v.rearrange("p (a b) -> p a b", b=dims[1])
            if len(dims) == 3:
                v = v.rearrange("p (a b c) -> p a b c", b=dims[1], c=dims[2])
            return v

        def flat(v):
            return v.rearrange("p a b -> p (a b)")

        def halves(b, n=S):
            return bank[b][:, :].rearrange("p (a b) -> p a b", b=n)

        def column(name, n=0):
            c = COL[name] + n
            return col[:, c:c + 1]

        ident, ones = const("ident"), const("ones")

        w_in = [sem(f"w_in{i}") for i in range(RING)]
        w_used = [sem(f"w_used{i}") for i in range(RING)]
        full = [sem(f"full{i}") for i in range(8)]
        free = [sem(f"free{i}") for i in range(8)]
        dve_step, act_step, pool_step = sem("dve_step"), sem("act_step"), sem("pool_step")
        vec_in, cst_in, x_in, small_in = sem("vec_in"), sem("cst_in"), sem("x_in"), sem("small_in")
        x_ready = sem("x_ready")
        h_ready = sem("h_ready")
        sq_ready = sem("sq_ready")
        std_ready = sem("std_ready")
        scaled = sem("scaled")
        up_full = sem("up_full")
        silu_done = sem("silu_done")
        hid_ready = sem("hid_ready")
        y_full = sem("y_full")
        out_done = sem("out_done")

        named = {}

        def sig(name):
            if name not in named:
                named[name] = sem(name)
            return named[name]

        def cumulative(stages):
            at, n = {}, 0
            for name, count in stages:
                n += count
                at[name] = n
            return at

        X_WRITES = [("init", 4), ("ffn0", 4), ("mix0", 4), ("ffn1", 4), ("ple0", 4), ("ffn2", 4),
                    ("mix1", 4), ("ffn3", 4), ("ple1", 4), ("between", 12),
                    ("even", 16), ("moe0", 16), ("odd", 8), ("moe1", 8)]
        X_AT = cumulative(X_WRITES)
        NORMS = [("ffn0", 8), ("mix0", 8), ("ffn1", 8), ("ple0", 8), ("ffn2", 8), ("mix1", 8), ("ffn3", 8),
                 ("ple1", 8), ("between", 0), ("even", 16), ("moe0", 16), ("odd", 16), ("moe1", 8), ("final", 8)]
        H_AT = cumulative(NORMS)
        NORM_NO = {name: n for n, (name, _) in enumerate(NORMS)}
        tiles = {}

        def filled(eng, name, i=None):
            b, n, step, _ = tiles[name]
            eng.wait_ge(full[b], n + 1 if i is None else n + 1 + step * i)
            return b

        def emptied(eng, name, i=None):
            b, _, step, n = tiles[name]
            eng.wait_ge(free[b], n + 1 if i is None else n + 1 + step * i)

        SQ = area(0, KT, 2 * S)
        STD, RSTD = area(4096, 2 * S), area(4608, 2 * S)
        HID = [area(5120 + 512 * i, 2 * S) for i in range(2)]
        SIL = [area(6144 + 512 * i, 2 * S) for i in range(2)]
        XIN = area(0, 2, D)
        PIN = area(2048, 4, 256)
        ROWS_IN = area(3072, 3, P)

        def PT(l):
            return XC[:, 2 * l:2 * l + 2, S:2 * S]

        GT = area(8192, 4, 512)
        SC = H[:, :, S:S + 32]
        APART = XC[:, 4:8, S:2 * S]

        LR, GUP = area(0, S), area(17444, S)
        Q0, K0, V0 = area(512, 2, S), area(1024, 2, S), area(1536, 2, 512)
        G0, XR, XG = area(2560, 4, S), area(3584, 4, S + 3), area(4620, 4, S)
        Z0, L0, CUM0, KD0 = area(5644, 2, S), area(6156, 2, S), area(6668, 2, S), area(7180, 2, S)
        OSQ0, ORS0 = area(5644, 4, S), area(6668, 4, S)
        KTOK0, TOT0 = area(7692, 2, S), area(8204, 8)
        ST0, O0 = area(8212, NCH * 2, P), area(9236, 4, S)
        XV, RA, IX, AA, TH, U0 = [area(10260 + 1024 * n, 4, S) for n in range(6)]
        WBD = area(16404, 8, P)
        LC = area(17428, 16)
        Z1, T1, T2, KK1, Q1 = [area(2048 * n, 8, S) for n in range(5)]
        V1, G1 = area(10240, 2, D), area(12288, 8, S)
        ST1 = area(14336, NCH * 8, P)
        KTOK1 = area(0, 2, D)
        TOT1, LB = area(18432, 32), area(18464, 9, KT)

        CA = area(19296, KT, 2)
        LAM = area(19312, 4)
        LOGG = area(19316, 8)
        CTXIN = area(12288, 2, D)
        HOT = area(14336, GRID * GRID)
        NB = area(8192, GRID * GRID)
        RPBT = area(18432, 56)
        QD, KD, VD = area(0, 4, 2 * S), area(2048, 4, 2 * S), area(4096, 4, 512)
        QN, KN, VN = area(6144, 4, 2 * S), area(8192, 4, 2 * S), area(10240, 4, 512)
        TB_E = area(12288, 640)
        ROT, COS, SIN = TB_E[:, 0:128], TB_E[:, 128:384], TB_E[:, 384:640]
        TMP = area(12928, 4, S)
        PR_E, AT_E = area(13952, 4, 512), area(16000, 8, S)
        ST_E = area(18048, 64)
        NBT = area(18112, 4, S)
        YSQ, YRS = area(0, 4, 2 * S), area(2048, 4, 2 * S)
        KM, QM, VM = area(0, 8, 512), area(4096, 8, S), area(6144, 4, 512)
        RQ, RK, RV, RG = area(8192, 2, S), area(8704, 2, 2 * S), area(9728, 4, 512), area(11776, 4, S)
        CQ, CKV, KR = area(12800, 2, S), area(13312, 512), area(13824, 512)
        PR_O, AT_O = area(12800, 4, 512), area(15360, 8, S)
        CSQ = area(14336, 1024)
        QTMP = area(15360, 2, 2, S)
        DT, DT2, SD = area(14336, 4, S), area(15360, 2, S), area(15872, 4, S)
        TB_O = area(17408, 640)
        ROTM, COSM, SINM = TB_O[:, 0:128], TB_O[:, 128:384], TB_O[:, 384:640]
        ST_O = area(18048, 64)
        RO, ROSQ, RORS = area(0, 4, S), area(1024, 4, S), area(2048, 4, S)
        XE = area(0, KT, 2 * NE * CAP)
        XE1 = area(0, KT, NE * CAP)
        TM, MACC = area(8192, 4, D), area(8192, KT, 2 * S)
        LG, AF, LMX = area(12288, 4, NE), area(12352, 4, NE), area(12416, 8)
        AFT, TV, TI, TIF = area(12424, 512), area(12936, 2, CAP), area(13000, 2, CAP), area(13064, 2, CAP)
        LGT = AFT
        BD = area(13128, 1024)
        IREP, GREP, IC, GC = area(14152, P), area(14280, P), area(14408, NE), area(14424, NE)
        PM, IOF = area(14464, 4, 512), area(16512, 512)
        P1, P3, YS, PG = area(14464, D), area(15488, D), area(12416, D), area(13440, 512)
        HIDT, SILT, XCUR = area(17024, 512), area(17536, 512), area(18048, 512)
        OUTT = area(8192, 2, D)

        nb_dram = nc.dram_tensor("na_bias", (8, 7, GRID, GRID), F32, kind="Internal").ap()

        ada_in, ctx_in, hot_in, nb_in = sem("ada_in"), sem("ctx_in"), sem("hot_in"), sem("nb_in")
        mx_ready = sem("mx_ready")
        exp_done = sem("exp_done")
        a_ready = sem("a_ready")
        xcur_ready, pg_ready = sem("xcur_ready"), sem("pg_ready")

        UNITS = {
            "diff": [(h, s, qt) for h in range(4) for s in range(2) for qt in range(2)],
            "na": [(h, s, qt) for h in range(8) for s in range(2) for qt in range(2)],
            "mla": [(h, 0, qt) for h in range(8) for qt in range(2)],
        }
        UNITS_BEFORE = {"diff": 0, "na": len(UNITS["diff"]), "mla": len(UNITS["diff"]) + len(UNITS["na"])}

        def key_range(kind, s):
            return (0, 2 * S) if s == 0 else (S, 2 * S)

        DEPTH = {"diff": 2, "na": 4, "mla": 4}

        def probs(kind, u, c=0):
            if kind == "diff":
                return PR_E[:, 2 * (u % 2) + c, :]
            return (PR_O if kind == "mla" else PR_E)[:, u % 4, :]

        def probs_T(kind, pair):
            a = AT_O if kind == "mla" else AT_E
            return a[:, 4 * (pair % 2):4 * (pair % 2) + 4, :]

        def experts(l):
            ns = 2 if l == 0 else 1
            return ns, ns * CAP, P // (ns * CAP), ns * S

        def xe_view(l, s, k):
            if l == 0:
                return XE[:, k, :].rearrange("p (e s c) -> p e s c", s=2, c=CAP)[:, :, s, :]
            return XE1[:, k, :].rearrange("p (e c) -> p e c", c=CAP)

        block = ctx.enter_context(nc.Block())

        @block.tensor
        def _(pe):
            fills, takes = [0] * 8, [0] * 8
            loads = Ring()
            held = []

            def mm(o, lhsT, rhs, start, stop, signal=None):
                ins = pe.matmul(o, lhsT, rhs, start=start, stop=stop, skip_group_check=True)
                if signal is not None:
                    ins.then_inc(signal, 1)
                elif held:
                    ins.then_inc(w_used[held.pop()], 1)

            def turn(o, src, signal=None):
                n = src.shape[0]
                ins = pe.transpose(o, src, ident[0:n, 0:n])
                if signal is not None:
                    ins.then_inc(signal, 1)
                elif held:
                    ins.then_inc(w_used[held.pop()], 1)

            def settle(b):
                if takes[b]:
                    pe.wait_ge(free[b], takes[b])

            def fill(name, b, i=None, step=0, counted=True):
                tiles[name] = (b, fills[b], step, takes[b])
                if i is not None:
                    pe.wait_ge(free[b], takes[b] + step * i)
                elif takes[b]:
                    pe.wait_ge(free[b], takes[b])
                fills[b] += 1
                takes[b] += counted
                return b

            def chunk(*dims):
                s, n = loads.next()
                pe.wait_ge(w_in[s], 16 * n + 16)
                held_next.append(s)
                v = ring[:, s, 0:int(np.prod(dims))]
                return v.rearrange("p (a b) -> p a b", b=dims[1]) if len(dims) == 2 else v

            held_next = []

            def done_with_chunk():
                held.append(held_next.pop(0))

            BANK7_AFTER = {"ffn2": "ple0", "between": "ple1", "moe0": "even"}

            def norm_sum(name, n):
                if name in BANK7_AFTER:
                    pe.wait_ge(x_ready, X_AT[BANK7_AFTER[name]])
                fill(f"norm.{name}", 7)
                for k in range(KT):
                    pe.wait_ge(sq_ready, 8 * NORM_NO[name] + k + 1)
                    mm(bank[7][:, 0:n], ones, SQ[:, k, 0:n], k == 0, k == KT - 1,
                       full[7] if k == KT - 1 else None)

            def features(name, banks, n, rhs=H, cols=256, first=None, kt=KT, counted=True):
                w = chunk(kt, cols)
                per = 512 // n
                for j in range(-(-cols // P)):
                    m = min(P, cols - j * P)
                    b = banks[j // per]
                    if j % per == 0:
                        fill(f"{name}{j // per}" if len(banks) > 1 else name, b, counted=counted)
                    last = j % per == per - 1 or (j + 1) * P >= cols
                    for k in range(kt):
                        if first is not None and j == 0:
                            pe.wait_ge(h_ready, first + k + 1 if n == S else first + 2 * k + 2)
                        mm(bank[b][0:m, (j % per) * n:(j % per) * n + n], w[:, k, j * P:j * P + m],
                           rhs[:, k, 0:n], k == 0 and j % per == 0, k == kt - 1,
                           full[b] if last and k == kt - 1 else None)
                done_with_chunk()

            def tokens(name, banks, ntiles, rhs=H, cols=256, at=0, kt=KT, free_it=True, w=None, first=None):
                w = chunk(kt, cols) if w is None else w
                for t in range(ntiles):
                    b = banks[t // 2]
                    if t % 2 == 0:
                        fill(f"{name}{t // 2}" if len(banks) > 1 else name, b)
                    for k in range(kt):
                        mm(bank[b][:, (t % 2) * cols:(t % 2 + 1) * cols], rhs[:, k, t * P:(t + 1) * P],
                           w[:, k, 0:cols], k == 0 and t % 2 == 0, k == kt - 1,
                           full[b] if t % 2 == 1 and k == kt - 1 else None)
                if free_it:
                    done_with_chunk()

            parts = [0]

            def modulation(a, b, g):
                n = parts[0]
                parts[0] += 1
                if n:
                    emptied(pe, f"ada{n - 1}a")
                    emptied(pe, f"ada{n - 1}b")
                    g = fill(f"mod{n - 1}", g)
                    for f in range(KT):
                        mm(bank[g][:, 2 * f:2 * f + 2], APART[:, f // 2, (f % 2) * P:(f % 2 + 1) * P],
                           const("sel4")[:, 0:2], f == 0, True, full[g] if f == KT - 1 else None)
                else:
                    pe.wait_ge(sig("sc_ready"), 1)
                if n == 12:
                    return
                ws = [chunk(2, D) for _ in range(4)]
                for half, name in enumerate("ab"):
                    o = fill(f"ada{n}{name}", (a, b)[half])
                    for kk in range(2):
                        for q in range(4):
                            mm(bank[o][32 * q:32 * q + 32, :], SC[:, 2 * q + kk, :],
                               ws[q][:, kk, half * 512:(half + 1) * 512], kk == 0, kk == 1,
                               full[o] if kk == 1 and q == 3 else None)
                for _ in range(4):
                    done_with_chunk()

            def feed_forward(f):
                norm_sum(f"ffn{f}", S)
                if f:
                    modulation(0, 1, 2)
                first = H_AT[f"ffn{f}"] - 8
                for b in range(4, 8):
                    settle(b)

                def up(s, i=0, after=True):
                    if after:
                        pe.wait_ge(hid_ready, FSTEPS * f + s - 1 + 4 * i)
                    for half in range(2):
                        w = chunk(KT, 256)
                        b = 4 + 2 * (s % 2) + half
                        for j in range(2):
                            for k in range(KT):
                                if s == 0 and half == 0 and j == 0:
                                    pe.wait_ge(h_ready, first + k + 1)
                                mm(bank[b][:, j * S:(j + 1) * S], w[:, k, j * P:(j + 1) * P], H[:, k, 0:S],
                                   j == 0 and k == 0, k == KT - 1,
                                   up_full if j == 1 and k == KT - 1 else None)
                        done_with_chunk()

                def down(s, i=0):
                    w = chunk(2, D)
                    pe.wait_ge(hid_ready, FSTEPS * f + s + 1 + 4 * i)
                    if s == 0:
                        for b in range(4):
                            settle(b)
                    for kk in range(2):
                        for m in range(KT):
                            end = s == FSTEPS - 1 and kk == 1
                            mm(bank[m // 2][:, (m % 2) * S:(m % 2 + 1) * S], w[:, kk, m * P:(m + 1) * P],
                               HID[s % 2][:, kk * S:(kk + 1) * S], s == 0 and kk == 0 and m % 2 == 0, end,
                               y_full if end and m == KT - 1 else None)
                    done_with_chunk()

                up(0, after=False)
                up(1, after=False)
                down(0)
                assert len(held) == 1
                with pe.Fori(0, 2) as i:
                    loads.loop(i)
                    for j in range(4):
                        up(2 + j, i)
                        down(1 + j, i)
                loads.end(2)
                up(FSTEPS - 1)
                down(FSTEPS - 2)
                down(FSTEPS - 1)

            pe.wait_ge(cst_in, 16)
            pe.wait_ge(vec_in, 16 * sum(len(v) for v, _, _ in VEC_GROUPS))
            for n, (_, _, rows) in enumerate(VEC_GROUPS):
                fill(f"vec{n}", n)
                turn(bank[n][:, 0:rows], ROWS_IN[0:rows, n, :], full[n])
            pe.wait_ge(x_in, 48)

            def turn_tokens(name, b0, src):
                for t in range(2):
                    for g in range(2):
                        b = fill(f"{name}{t}{g}", b0 + 2 * t + g, counted=False)
                        for k in range(4):
                            turn(bank[b][:, k * P:(k + 1) * P], src[:, t, (4 * g + k) * P:(4 * g + k + 1) * P],
                                 full[b] if k == 3 else None)

            for l in range(2):
                b = fill(f"p{l}", (7, 0)[l])
                for t in range(2):
                    for k in range(2):
                        turn(bank[b][:, (2 * t + k) * P:(2 * t + k + 1) * P], PIN[:, 2 * l + t, k * P:(k + 1) * P],
                             full[b] if t == 1 and k == 1 else None)

            turn_tokens("x", 3, XIN)

            def out_projection(name, ready, n, count=4):
                for c in range(4):
                    if c == 0:
                        pe.wait_ge(ready, count)
                    features(f"{name}.out{c}" if n == S else f"{name}.out{c}.", [c] if n == S else [2 * c, 2 * c + 1], n,
                             counted=False)

            def mixer0():
                norm_sum("mix0", S)
                modulation(5, 6, 4)
                first = H_AT["mix0"] - 8
                features("lr", [0], S, cols=16, first=first)
                features("k0", [1], S)
                features("q0", [2], S)
                tokens("v0a", [3], 2)
                tokens("v0b", [4], 2)
                emptied(pe, "lr")
                pe.wait_ge(small_in, 16 * 5)
                b = fill("gate", 5)
                for j in range(2):
                    mm(bank[b][:, j * S:(j + 1) * S], GUP[0:16, j * P:(j + 1) * P], LR[0:16, :],
                       j == 0, True, full[b] if j == 1 else None)
                features("xr0", [6], S)
                features("xr1", [7], S)
                features("g0a", [0], S)
                features("g0b", [1], S)
                features("xg0", [2], S)
                features("xg1", [3], S)
                modulation(6, 7, 5)
                pe.wait_ge(sig("kdec0"), 1)
                b = fill("kdT", 4)
                for t in range(2):
                    for j in range(2):
                        turn(bank[b][:, t * S + j * P:t * S + (j + 1) * P], KD0[:, j, t * P:(t + 1) * P],
                             full[b] if t == 1 and j == 1 else None)
                emptied(pe, "kdT")
                emptied(pe, "v0a")
                emptied(pe, "v0b")
                for c in range(NCH):
                    t, r = c // 2, CH * (c % 2)
                    b = fill(f"kv0.{c}", (5, 0, 6, 1)[c])
                    for j in range(2):
                        mm(bank[b][:, j * S:(j + 1) * S], KTOK0[r:r + CH, t, j * P:(j + 1) * P],
                           V0[r:r + CH, t, j * S:(j + 1) * S], j == 0, True, full[b] if j == 1 else None)
                pe.wait_ge(sig("conv"), 1)
                for n in range(4):
                    b = fill(f"lru{n}", (7, 2, 3, 4)[n])
                    for j in range(2):
                        i = 2 * (n % 2) + j
                        mm(bank[b][:, j * S:(j + 1) * S], WBD[:, 4 * (n // 2) + i, :], XV[:, i, :],
                           j == 0, True, full[b] if j == 1 else None)
                emptied(pe, "kv0.3")
                emptied(pe, "q0")
                for par in range(2):
                    b = fill(f"o0.{par}", (5, 6)[par])
                    for j in range(2):
                        for c in range(NCH):
                            mm(bank[b][:, j * S + c * CH:j * S + (c + 1) * CH], ST0[par * 64:par * 64 + 64, 2 * c + j, :],
                               Q0[par * 64:par * 64 + 64, j, c * CH:(c + 1) * CH], j == 0 and c == 0, True,
                               full[b] if j == 1 and c == NCH - 1 else None)
                modulation(7, 2, 3)
                pe.wait_ge(sig("osq0"), 1)
                for n in range(2):
                    b = fill(f"on0.{n}", n)
                    mm(bank[b][:, :], ones, flat(OSQ0)[:, n * 512:(n + 1) * 512], True, True, full[b])
                modulation(4, 5, 6)
                out_projection("mix0", sig("y0_ready"), S, 2)

            def mixer1():
                norm_sum("mix1", S)
                modulation(5, 6, 4)
                first = H_AT["mix1"] - 8
                for c in range(4):
                    features(f"z1.{c}", [c], S, first=first if c == 0 else None)
                for c in range(4):
                    tokens(f"v1.{c}", [4 + c], 2)
                for c in range(4):
                    features(f"q1.{c}", [c], S)
                for c in range(4):
                    features(f"g1.{c}", [4 + c], S)
                modulation(2, 3, 1)
                pe.wait_ge(sig("kdec1"), 1)
                for t in range(2):
                    for g in range(2):
                        b = fill(f"kdT1.{t}{g}", 2 * t + g)
                        for j in range(4):
                            turn(bank[b][:, j * P:(j + 1) * P], T2[:, 4 * g + j, t * P:(t + 1) * P],
                                 full[b] if j == 3 else None)
                for t in range(2):
                    for g in range(2):
                        emptied(pe, f"kdT1.{t}{g}")
                for c in range(4):
                    emptied(pe, f"v1.{c}")
                for c in range(NCH):
                    t, r = c // 2, CH * (c % 2)
                    for g in range(2):
                        b = fill(f"kv1.{c}{g}", 2 * c + g)
                        for j in range(4):
                            h = 4 * g + j
                            mm(bank[b][:, j * P:(j + 1) * P], KTOK1[r:r + CH, t, h * P:(h + 1) * P],
                               V1[r:r + CH, t, h * P:(h + 1) * P], j == 0, True, full[b] if j == 3 else None)
                for c in range(4):
                    emptied(pe, f"q1.{c}")
                for g in range(2):
                    emptied(pe, f"kv1.3{g}")
                for g in range(4):
                    b = fill(f"o1.{g}", g)
                    for j in range(2):
                        for c in range(NCH):
                            mm(bank[b][:, j * S + c * CH:j * S + (c + 1) * CH], ST1[:, 8 * c + 2 * g + j, :],
                               Q1[:, 2 * g + j, c * CH:(c + 1) * CH], j == 0 and c == 0, True,
                               full[b] if j == 1 and c == NCH - 1 else None)
                modulation(4, 5, 6)
                pe.wait_ge(sig("osq1"), 1)
                for g in range(4):
                    b = fill(f"on1.{g}", 4 + g)
                    mm(bank[b][:, :], ones, flat(T2)[:, g * 512:(g + 1) * 512], True, True, full[b])
                modulation(4, 5, 6)
                out_projection("mix1", sig("y1_ready"), S, 1)

            def ple(l):
                norm_sum(f"ple{l}", S)
                modulation(4, 5, 6)
                first = H_AT[f"ple{l}"] - 8
                for c in range(4):
                    features(f"pg{l}.{c}", [c], S, first=first if c == 0 else None)
                w = chunk(2, D)
                for c in range(4):
                    b = fill(f"pp{l}.{c}", 4 + c, counted=False)
                    for j in range(2):
                        for k in range(2):
                            mm(bank[b][:, j * S:(j + 1) * S], w[:, k, (2 * c + j) * P:(2 * c + j + 1) * P],
                               PT(l)[:, k, :], j == 0 and k == 0, k == 1, full[b] if j == 1 and k == 1 else None)
                done_with_chunk()

            def idle_products(b):
                settle(b)
                while held:
                    mm(bank[b][:, 0:2], ones, ones[:, 0:2], True, True)

            def block2_pe():
                norm_sum("between", S)
                pe.wait_ge(ctx_in, 16)
                turn_tokens("ctx", 0, CTXIN)
                pe.wait_ge(hot_in, 16 * 9)
                for n in range(8):
                    if n == 4:
                        pe.wait_ge(x_ready, X_AT["between"] - KT)
                    b = fill(f"hot{n}", (n + 4) % 8)
                    for j in range(2):
                        mm(bank[b][0:56, j * S:(j + 1) * S], RPBT[0:32, :], HOT[0:32, n * 512 + j * S:n * 512 + (j + 1) * S],
                           j == 0, True, full[b] if j == 1 else None)

                def attention(kind, query, keys, values, row, after_output=None):
                    units = UNITS[kind]
                    comps = 2 if kind == "diff" else 1

                    def scores(u):
                        h, s, qt = units[u]
                        for c in range(comps):
                            b = fill(f"{kind}.s{u}.{c}", 2 * (u % 2) + c if comps == 2 else u % 4)
                            k0, k1 = key_range(kind, s)
                            q = query(h, c)[:, s * S + qt * P:s * S + (qt + 1) * P]
                            mm(bank[b][:, 0:k1 - k0], q, keys(h, c)[:, k0:k1], True, True, full[b])

                    def turns(u):
                        _, s, _ = units[u]
                        pe.wait_ge(a_ready, UNITS_BEFORE[kind] + u + 1)
                        b = fill(f"{kind}.t{u}", 4 + u % 2)
                        n = 4 if s == 0 else 2
                        for kt in range(n):
                            turn(bank[b][:, kt * P:(kt + 1) * P], probs(kind, u)[:, kt * P:(kt + 1) * P],
                                 full[b] if kt == n - 1 else None)

                    def output(pair):
                        h, s, _ = units[2 * pair]
                        emptied(pe, f"{kind}.t{2 * pair}")
                        emptied(pe, f"{kind}.t{2 * pair + 1}")
                        b = fill(f"{kind}.o{pair}", 6 + pair % 2)
                        n = 4 if s == 0 else 2
                        r0, r1 = row(h)
                        for kt in range(n):
                            mm(bank[b][r0:r1, 0:S], values(h, kt + (0 if s == 0 else 2)),
                               probs_T(kind, pair)[:, kt, :], kt == 0, kt == n - 1, full[b] if kt == n - 1 else None)

                    ahead = 2 if comps == 2 else 3
                    for u in range(ahead):
                        scores(u)
                    for u in range(len(units)):
                        if u + ahead < len(units):
                            scores(u + ahead)
                        turns(u)
                        if u >= 2 and u % 2 == 0:
                            output(u // 2 - 1)
                            if after_output is not None:
                                after_output(u // 2 - 1)
                    output(len(units) // 2 - 1)

                def even():
                    norm_sum("even", 2 * S)
                    first = H_AT["even"] - 16
                    for c, name in enumerate(("qd0", "qd1", "kd0", "kd1")):
                        features(f"{name}.", [2 * c, 2 * c + 1], 2 * S, first=first if c == 0 else None)
                    for c, name in enumerate(("vd0", "vd1")):
                        tokens(f"{name}.", [2 * c, 2 * c + 1], 4)
                    emptied(pe, "qd1.1")
                    for n in range(2):
                        emptied(pe, f"qd{n}.0")
                        emptied(pe, f"qd{n}.1")
                        emptied(pe, f"kd{n}.0")
                        emptied(pe, f"kd{n}.1")
                    pe.wait_ge(sig("tb_e"), 16)
                    for n, (name, src) in enumerate((("rq0", QD[:, 0:2]), ("rq1", QD[:, 2:4]), ("rk0", KD[:, 0:2]),
                                                     ("rk1", KD[:, 2:4]))):
                        b = fill(name, (5, 6, 7, 4)[n])
                        for j in range(2):
                            mm(bank[b][:, j * S:(j + 1) * S], ROT, src[:, j, 0:S], j == 0, True,
                               full[b] if j == 1 else None)
                    for c, name in enumerate(("qn0", "qn1", "kn0", "kn1")):
                        features(f"{name}.", [2 * (c % 2), 2 * (c % 2) + 1], 2 * S)
                    for c, name in enumerate(("vn0", "vn1")):
                        tokens(f"{name}.", [4 + 2 * c, 5 + 2 * c], 4)
                    idle_products(0)
                    for name in ("vd0.0", "vd0.1", "vd1.0", "vd1.1"):
                        emptied(pe, name)
                    pe.wait_ge(sig("rope"), 2)
                    attention("diff", lambda h, c: QD[64 * c:64 * c + 64, h, :], lambda h, c: KD[64 * c:64 * c + 64, h, :],
                              lambda h, kt: VD[:, kt, h * P:(h + 1) * P], lambda h: (0, P))
                    for name in ("qn0.0", "qn0.1", "qn1.0", "qn1.1", "kn0.0", "kn0.1", "kn1.0", "kn1.1",
                                 "vn0.0", "vn0.1", "vn1.0", "vn1.1"):
                        emptied(pe, name)

                    def head_norm(pair):
                        h = pair - 4
                        if 0 <= h < 4:
                            pe.wait_ge(sig("ysq"), h + 1)
                            b = fill(f"yn{h}", 6 + (pair + 1) % 2)
                            mm(bank[b][:, :], ones, YSQ[:, h, :], True, True, full[b])

                    attention("na", lambda h, c: QN[64 * (h % 2):64 * (h % 2) + 64, h // 2, :],
                              lambda h, c: KN[64 * (h % 2):64 * (h % 2) + 64, h // 2, :],
                              lambda h, kt: VN[:, kt, h * 64:(h + 1) * 64],
                              lambda h: (64 * (h % 2), 64 * (h % 2) + 64), head_norm)
                    emptied(pe, "na.o14")
                    emptied(pe, "na.o15")
                    out_projection("even", sig("ye_ready"), 2 * S, 4)

                def odd():
                    norm_sum("odd", 2 * S)
                    pe.wait_ge(h_ready, H_AT["odd"])
                    features("cq", [0], S)
                    w = chunk(KT, 160)
                    b = fill("ckv", 1)
                    for k in range(KT):
                        mm(bank[b][:, :], w[:, k, 0:P], H[:, k, :], k == 0, k == KT - 1, full[b] if k == KT - 1 else None)
                    b = fill("kr", 2)
                    for k in range(KT):
                        mm(bank[b][64:96, :], w[:, k, P:P + 32], H[:, k, :], k == 0, k == KT - 1,
                           full[b] if k == KT - 1 else None)
                    done_with_chunk()
                    features("rq", [3], S)
                    features("rk.", [4, 5], 2 * S)
                    tokens("rv0.", [6, 7], 4)
                    pe.wait_ge(sig("csq"), 2)
                    b = fill("cqn", 0)
                    for j in range(2):
                        mm(bank[b][:, 0:S], ones, CSQ[:, j * S:(j + 1) * S], j == 0, j == 1, full[b] if j == 1 else None)
                    b = fill("ckvn", 1)
                    mm(bank[b][:, :], ones, CSQ[:, 512:1024], True, True, full[b])
                    tokens("rv1.", [2, 3], 4)
                    features("rg0", [4], S)
                    features("rg1", [5], S)
                    w = chunk(2, 768)
                    pe.wait_ge(sig("latents"), 2)
                    for n in range(4):
                        b = fill(f"qm{n}", (6, 7, 0, 1)[n])
                        for j in range(2):
                            h = 2 * n + j
                            for k in range(2):
                                mm(bank[b][0:96, j * S:(j + 1) * S], w[:, k, h * 96:(h + 1) * 96], CQ[:, k, :],
                                   j == 0 and k == 0, k == 1, full[b] if j == 1 and k == 1 else None)
                    done_with_chunk()
                    pe.wait_ge(sig("tb_o"), 16)
                    emptied(pe, "kr")
                    b = fill("krr", 2)
                    for j in range(2):
                        mm(bank[b][64:96, j * P:(j + 1) * P], ROTM[64:96, 64:96], KR[64:96, j * P:(j + 1) * P], j == 0, True,
                           full[b] if j == 1 else None)
                    for n in range(4):
                        emptied(pe, f"qm{n}")
                    for n in range(4):
                        b = fill(f"qr{n}", (3, 4, 5, 6)[n])
                        for j in range(2):
                            mm(bank[b][0:96, j * S:(j + 1) * S], ROTM[0:96, 0:96], QM[0:96, 2 * n + j, :], j == 0, True,
                               full[b] if j == 1 else None)
                    w = chunk(1, D)[:, 0, :].rearrange("p (h a) -> p h a", a=P)
                    for h in range(8):
                        b = fill(f"kn.{h}", (7, 0, 1, 2)[h % 4])
                        for j in range(2):
                            mm(bank[b][0:64, j * S:(j + 1) * S], w[:, h, 0:64], CKV[:, j * S:(j + 1) * S], j == 0, True,
                               full[b] if j == 1 else None)
                    for t in range(4):
                        b = fill(f"vm{t}", (3, 4, 5, 6)[t])
                        for j in range(2):
                            mm(bank[b][:, j * S:(j + 1) * S], CKV[:, t * P:(t + 1) * P], w[:, 4 * j:4 * j + 4, 64:P],
                               j == 0, True, full[b] if j == 1 else None)
                    done_with_chunk()
                    for h in range(8):
                        emptied(pe, f"kn.{h}")
                    for t in range(4):
                        emptied(pe, f"vm{t}")
                    pe.wait_ge(sig("rope_m"), 1)
                    for n in range(4):
                        emptied(pe, f"qr{n}")
                    idle_products(7)
                    attention("mla", lambda h, c: QM[0:96, h, :], lambda h, c: KM[0:96, h, :],
                              lambda h, kt: VM[:, kt, h * 64:(h + 1) * 64],
                              lambda h: (64 * (h % 2), 64 * (h % 2) + 64))
                    for name in ("rq", "rk.0", "rk.1", "rv0.0", "rv0.1", "rv1.0", "rv1.1"):
                        emptied(pe, name)

                    def ret_scores(h):
                        r, j = 64 * (h % 2), h // 2
                        for n in range(2):
                            b = fill(f"rs{h}.{n}", 2 * (h % 2) + n)
                            for i in range(2):
                                kt = 2 * n + i
                                mm(bank[b][:, i * S:(i + 1) * S], RK[r:r + 64, j, kt * P:(kt + 1) * P], RQ[r:r + 64, j, :],
                                   i == 0, True, full[b] if i == 1 else None)

                    ret_scores(0)
                    for h in range(4):
                        if h < 3:
                            ret_scores(h + 1)
                        emptied(pe, f"rs{h}.0")
                        emptied(pe, f"rs{h}.1")
                        b = fill(f"ro{h}", 4 + h)
                        for kt in range(4):
                            mm(bank[b][:, 0:S], RV[:, kt, h * P:(h + 1) * P], SD[:, kt, :], kt == 0, kt == 3,
                               full[b] if kt == 3 else None)
                    pe.wait_ge(sig("rosq"), 1)
                    for n in range(2):
                        b = fill(f"rn{n}", n)
                        mm(bank[b][:, :], ones, flat(ROSQ)[:, n * 512:(n + 1) * 512], True, True, full[b])
                    out_projection("odd", sig("yo_ready"), S, 1)

                def moe(l):
                    ns, slots, groups, nt = experts(l)
                    norm_sum(f"moe{l}", nt)
                    w = chunk(KT, NE)
                    b = fill(f"rw{l}", 0)
                    for k in range(KT):
                        pe.wait_ge(h_ready, H_AT[f"moe{l}"] - ns * (KT - 1 - k))
                        mm(bank[b][0:NE, 0:nt], w[:, k, :], H[:, k, 0:nt], k == 0, k == KT - 1,
                           full[b] if k == KT - 1 else None)
                    done_with_chunk()
                    emptied(pe, f"rw{l}")
                    b = fill(f"rt{l}", 1)
                    for t in range(2 * ns):
                        turn(bank[b][:, t * NE:(t + 1) * NE], LGT[0:NE, t * P:(t + 1) * P],
                             full[b] if t == 2 * ns - 1 else None)
                    for t in range(2 * ns):
                        for g in range(2):
                            b = fill(f"tm{l}.{t}{g}", 2 + (2 * t + g) % 4)
                            for k in range(4):
                                turn(bank[b][:, k * P:(k + 1) * P], H[:, 4 * g + k, t * P:(t + 1) * P],
                                     full[b] if k == 3 else None)
                    pe.wait_ge(sig("aff_ready"), l + 1)
                    b = fill(f"aft{l}", 1)
                    for t in range(2 * ns):
                        turn(bank[b][0:NE, t * P:(t + 1) * P], AF[:, t, :], full[b] if t == 2 * ns - 1 else None)
                    pe.wait_ge(sig("top_ready"), l + 1)
                    for n in range(ns):
                        b = fill(f"ib{l}.{n}", 6 + n)
                        mm(bank[b][:, :], ones[0:NE, :], BD[0:NE, n * 512:(n + 1) * 512], True, True, full[b])
                    b = fill(f"ic{l}", 0)
                    mm(bank[b][:, 0:NE], IREP[0:NE, :], ident[0:NE, 0:NE], True, True)
                    mm(bank[b][:, NE:2 * NE], GREP[0:NE, :], ident[0:NE, 0:NE], False, True, full[b])
                    for n in range(ns):
                        emptied(pe, f"ib{l}.{n}")
                    emptied(pe, f"ic{l}")
                    for t in range(2 * ns):
                        for g in range(2):
                            emptied(pe, f"tm{l}.{t}{g}")
                    for s in range(ns):
                        for k in range(KT):
                            b = fill(f"xe{l}.{s}{k}", k)
                            for t in range(2):
                                mm(bank[b][:, :], TM[:, 2 * s + t, k * P:(k + 1) * P], PM[:, 2 * s + t, :], t == 0, t == 1,
                                   full[b] if t == 1 else None)

                    per_set = groups // 2
                    sel = const("sel2" if slots == 64 else "sel4")
                    STEP = [3, 3, 3, 3, 1, 1, 1, 1]

                    def by_weights(name, b0, left, i):
                        fill(f"{name}a", b0, i, STEP[b0])
                        fill(f"{name}b", b0 + 1, i, STEP[b0 + 1])
                        for q in range(0, 4, per_set):
                            ws = [chunk(2, D) for _ in range(per_set)]
                            for half in range(2):
                                for j, w in enumerate(ws):
                                    for kk in range(2):
                                        g = 2 * j + kk
                                        end = q + per_set == 4
                                        mm(bank[b0 + half][slots * g:slots * (g + 1), :],
                                           left[:, (2 * (q + j) + kk) * slots:(2 * (q + j) + kk + 1) * slots],
                                           w[:, kk, half * 512:(half + 1) * 512], q == 0, end,
                                           full[b0 + half] if end and g == groups - 1 else None)
                            for _ in ws:
                                done_with_chunk()

                    def add_groups(name, b, part, i):
                        fill(name, b, i, STEP[b])
                        for f in range(KT):
                            mm(bank[b][:, f * slots:(f + 1) * slots], part[:, f * P:(f + 1) * P], sel,
                               f == 0, True, full[b] if f == KT - 1 else None)

                    def scatter(pre, i, first):
                        emptied(pe, f"m{l}.p.ya", first)
                        emptied(pe, f"m{l}.p.yb", first)
                        pe.wait_ge(pg_ready, NE * l + 1 if first is None else NE * l + 1 + first)
                        for k in range(KT):
                            b = fill(f"{pre}f{k}", k % 4, i, STEP[k % 4])
                            mm(bank[b][:, 0:nt], YS[:, k * P:(k + 1) * P], PG[:, 0:nt], True, True, full[b])

                    def expert(pre, i):
                        pe.wait_ge(xcur_ready, NE * l + 1 if i is None else NE * l + 2 + i)
                        by_weights(f"{pre}h1", 0, XCUR, i)
                        by_weights(f"{pre}h3", 2, XCUR, i)
                        emptied(pe, f"{pre}h1a", i)
                        emptied(pe, f"{pre}h1b", i)
                        add_groups(f"{pre}s1", 4, P1, i)
                        emptied(pe, f"{pre}h3a", i)
                        emptied(pe, f"{pre}h3b", i)
                        add_groups(f"{pre}s3", 5, P3, i)
                        if i is not None:
                            scatter(pre, i, i)
                        emptied(pe, f"{pre}s3", i)
                        by_weights(f"{pre}y", 6, HIDT, i)
                        if i is None:
                            for half in "ab":
                                b, n, _, m = tiles[f"{pre}y{half}"]
                                tiles[f"{pre}y{half}"] = (b, n, 1, m)

                    expert(f"m{l}.p.", None)
                    with pe.Fori(0, NE - 1) as i:
                        loads.loop(i)
                        expert(f"m{l}.", i)
                    loads.end(NE - 1)
                    for b in range(8):
                        fills[b] += STEP[b] * (NE - 2)
                        takes[b] += STEP[b] * (NE - 2)
                    idle_products(5)
                    scatter(f"m{l}.z.", None, NE - 1)

                even()
                moe(0)
                odd()
                moe(1)
                norm_sum("final", S)
                pe.wait_ge(h_ready, H_AT["final"])
                for t in range(2):
                    for g in range(2):
                        b = fill(f"out{t}{g}", 2 * t + g)
                        for k in range(4):
                            turn(bank[b][:, k * P:(k + 1) * P], H[:, 4 * g + k, t * P:(t + 1) * P],
                                 full[b] if k == 3 else None)

            feed_forward(0)
            mixer0()
            feed_forward(1)
            ple(0)
            feed_forward(2)
            mixer1()
            feed_forward(3)
            ple(1)
            block2_pe()

        @block.vector
        def _(dve):
            steps = [0]

            def step(ins):
                steps[0] += 1
                ins.then_inc(dve_step, 1)
                dve.wait_ge(dve_step, steps[0])

            def tt(o, a, b, op):
                return dve.tensor_tensor(o, a, b, op)

            def ts(o, a, s1, op0, s2=None, op1=ALU.bypass):
                return dve.tensor_scalar(o, a, s1, s2, op0, op1) if s2 is not None else dve.tensor_scalar(o, a, s1, None, op0)

            def stt(o, a, s, b, op0, op1):
                return dve.scalar_tensor_tensor(out=o, in0=a, scalar=s, in1=b, op0=op0, op1=op1)

            def take(name, o, view=None):
                b = filled(dve, name)
                v = halves(b) if view is None else view(bank[b])
                dve.tensor_copy(o, v).then_inc(free[b], 1)

            parts = [0]

            def modulation():
                n = parts[0]
                parts[0] += 1
                if n < 12:
                    take(f"ada{n}b", APART[:, 2:4, :])
                if n:
                    b = filled(dve, f"mod{n - 1}")
                    tt(MODS.rearrange("p l (v f) s -> p (l v) f s", f=KT)[:, n - 1],
                       bank[b][:, 0:16].rearrange("p (f s) -> p f s", s=2),
                       col[:, COL["ada_b_2"] + 8 * (n - 1):COL["ada_b_2"] + 8 * n].unsqueeze(2).to_broadcast([P, 8, 2]),
                       ALU.add).then_inc(free[b], 1)

            def rstd(name):
                dve.wait_ge(std_ready, NORM_NO[name] + 1)

            def norm(name, gains, g0):
                rstd(name)
                for k in range(KT):
                    stt(H[:, k, 0:S], XC[:, k, 0:S], column(gains, g0 + k), RSTD[:, 0:S],
                        ALU.mult, ALU.mult).then_inc(h_ready, 1)

            def feed_forward(f):
                norm(f"ffn{f}", "ffn_norm", 8 * f)
                if f:
                    modulation()

                def gate(s, i=0):
                    dve.wait_ge(silu_done, FSTEPS * f + s + 1 + 4 * i)
                    dve.wait_ge(up_full, 2 * (FSTEPS * f + s + 1) + 8 * i)
                    tt(HID[s % 2], SIL[s % 2], bank[5 + 2 * (s % 2)][:, :], ALU.mult).then_inc(hid_ready, 1)

                gate(0)
                gate(1)
                with dve.Fori(0, 2) as i:
                    for j in range(4):
                        gate(2 + j, i)
                gate(FSTEPS - 1)
                dve.wait_ge(y_full, f + 1)
                for b in range(4):
                    xs = XC[:, 2 * b:2 * b + 2, 0:S]
                    stt(xs, halves(b), 0.5, xs, ALU.mult, ALU.add).then_inc(x_ready, 1)

            def min0_minus(o, z, ln):
                return stt(o, z, 0.0, ln, ALU.min, ALU.subtract)

            def add_output(name):
                for c in range(4):
                    b = filled(dve, f"{name}.out{c}")
                    xs = XC[:, 2 * c:2 * c + 2, 0:S]
                    tt(xs, halves(b), xs, ALU.add).then_inc(x_ready, 1)

            for n, (_, start, rows) in enumerate(VEC_GROUPS):
                take(f"vec{n}", col[:, start:start + rows], lambda b: b[:, 0:rows])
            step(dve.memset(SC, 0.0))
            emptied(dve, "vec1")
            for n, name in enumerate(("c_2", "c_ctx_2")):
                ins = dve.tensor_copy(SC[:, :, n], col[:, COL[name]:COL[name] + 8])
            ins.then_inc(sig("sc_raw"), 1)
            for l in range(2):
                b = filled(dve, f"p{l}")
                dve.tensor_copy(PT(l).rearrange("p k (t n) -> p t k n", t=2),
                                bank[b][:, :].rearrange("p (t k n) -> p t k n", t=2, k=2)).then_inc(free[b], 1)

            for t in range(2):
                for g in range(2):
                    b = filled(dve, f"x{t}{g}")
                    dve.tensor_copy(XC[:, 4 * g:4 * g + 4, t * P:(t + 1) * P],
                                    halves(b, P)).then_inc(x_ready, 1)

            def mixer0():
                norm("mix0", "mix_norm", 0)
                modulation()
                lam = col[:, COL["lru_lambda"]:COL["lru_lambda"] + 4]
                dve.wait_ge(sig("lam_ln"), 1)
                step(min0_minus(LC[:, 0:4], lam, LC[:, 8:12]))
                step(ts(LC[:, 0:4], LC[:, 0:4], 8.0, ALU.mult))
                ts(LC[:, 4:8], LC[:, 0:4], -1.0, ALU.mult).then_inc(sig("lam_ready"), 1)
                take("lr", LR[0:16, :], lambda b: b[0:16, 0:S])
                take("k0", K0)
                b = filled(dve, "gate")
                ts(Z0[:, 0, :], bank[b][:, 0:S], column("gla_gate_bias", 0), ALU.add)
                ts(Z0[:, 1, :], bank[b][:, S:], column("gla_gate_bias", 1), ALU.add).then_inc(free[b], 1)
                step(dve.memset(XR[:, :, 0:3], 0.0))
                take("xr0", XR[:, 0:2, 3:])
                take("xr1", XR[:, 2:4, 3:])
                dve.wait_ge(sig("gate_ln"), 1)
                step(min0_minus(Z0, Z0, L0))
                step(ts(Z0, Z0, 1.0 / 16.0, ALU.mult))
                for j in range(2):
                    step(dve.tensor_tensor_scan(CUM0[:, j, :], const("reset"), Z0[:, j, :], 0.0, ALU.mult, ALU.add))
                cum = flat(CUM0).rearrange("p (c t) -> p c t", t=CH)
                tt(flat(L0).rearrange("p (c t) -> p c t", t=CH), cum[:, :, CH - 1:CH].to_broadcast([P, 2 * NCH, CH]),
                   cum, ALU.subtract).then_inc(sig("decay0"), 1)
                emptied(dve, "xr1")
                for tap in range(4):
                    for i in range(4):
                        w = column("lru_conv_w", 4 * tap + i)
                        if tap == 0:
                            ins = ts(XV[:, i, :], XR[:, i, 0:S], w, ALU.mult, column("lru_conv_b", i), ALU.add)
                        else:
                            ins = stt(XV[:, i, :], XR[:, i, tap:tap + S], w, XV[:, i, :], ALU.mult, ALU.add)
                        if i == 3 and tap < 3:
                            step(ins)
                ins.then_inc(sig("conv"), 1)
                modulation()
                dve.wait_ge(sig("decay_exp0"), 1)
                tt(KD0, K0, L0, ALU.mult).then_inc(sig("kdec0"), 1)
                take("kdT", KTOK0)
                for c in range(NCH):
                    b = filled(dve, f"kv0.{c}")
                    for j in range(2):
                        for r in (0, 64):
                            o = ST0[r:r + 64, 2 * c + j, :]
                            kv = bank[b][r:r + 64, j * S + 2 * r:j * S + 2 * r + P]
                            if c == 0:
                                ins = dve.tensor_copy(o, kv)
                            else:
                                ins = stt(o, ST0[r:r + 64, 2 * c - 2 + j, :], TOT0[r:r + 64, j * NCH + c:j * NCH + c + 1],
                                          kv, ALU.mult, ALU.add)
                    ins.then_inc(free[b], 1)
                    emptied(dve, f"kv0.{c}")
                for par in range(2):
                    take(f"o0.{par}", O0.rearrange("p (j r) n -> p r j n", r=2)[:, par])
                modulation()
                dve.wait_ge(sig("lru_exp"), 1)
                step(tt(U0, AA, AA, ALU.mult))
                stt(flat(U0), flat(U0), 1.0, flat(TH), ALU.add, ALU.mult).then_inc(sig("lru_arg"), 1)
                step(tt(IX, IX, XV, ALU.mult))
                dve.wait_ge(sig("lru_root"), 1)
                step(tt(U0, U0, IX, ALU.mult))
                for i in range(4):
                    ins = dve.tensor_tensor_scan(TH[:, i, :], AA[:, i, :], U0[:, i, :], 0.0, ALU.mult, ALU.add)
                step(ins)
                emptied(dve, "xg1")
                tt(H[:, 4:8, 0:S], TH, XG, ALU.mult).then_inc(sig("y0_ready"), 1)
                dve.wait_ge(sig("ostd0"), 1)
                step(tt(O0, O0, ORS0, ALU.mult))
                emptied(dve, "g0b")
                stt(H[:, 0:4, 0:S], O0, column("gla_head_norm"), G0, ALU.mult, ALU.mult).then_inc(sig("y0_ready"), 1)
                modulation()
                add_output("mix0")

            def mixer1():
                norm("mix1", "mix_norm", 8)
                modulation()
                l0, l1 = [col[:, COL["hgrn_lb_logits"] + 8 * n:COL["hgrn_lb_logits"] + 8 * n + 8] for n in range(2)]
                top, e0, e1, lb, om, ln_lb, ln_om, gap, _ = [LB[:, n, :] for n in range(9)]
                step(tt(top, l0, l1, ALU.max))
                tt(e0, l0, top, ALU.subtract)
                tt(e1, l1, top, ALU.subtract).then_inc(sig("lb_arg"), 1)
                dve.wait_ge(sig("lb_exp"), 1)
                step(tt(top, e0, e1, ALU.add))
                step(dve.reciprocal(top, top))
                step(tt(e0, e0, top, ALU.mult))
                step(tt(e1, e1, top, ALU.mult))
                step(tt(lb, e0, e1, ALU.add))
                step(tt(lb, lb, e0, ALU.subtract))
                ts(om, lb, -1.0, ALU.mult, 1.0, ALU.add).then_inc(sig("lb_ready"), 1)
                for c in range(4):
                    take(f"z1.{c}", Z1[:, 2 * c:2 * c + 2, :])
                dve.wait_ge(sig("ln1a"), 1)
                step(tt(gap, ln_om, ln_lb, ALU.subtract))
                min0_minus(flat(T1), flat(Z1), flat(T1)).then_inc(sig("ls1"), 1)
                dve.wait_ge(sig("ln1b"), 1)
                for k in range(KT):
                    ins = ts(T1[:, k, :], T1[:, k, :], ln_om[:, k:k + 1], ALU.add, ln_lb[:, k:k + 1], ALU.max)
                step(ins)
                step(tt(T1, T1, T2, ALU.add))
                for k in range(KT):
                    ins = dve.tensor_tensor_scan(T2[:, k, :], const("reset"), T1[:, k, :], 0.0, ALU.mult, ALU.add)
                step(ins)
                cum = flat(T2).rearrange("p (c t) -> p c t", t=CH)
                tt(flat(T1).rearrange("p (c t) -> p c t", t=CH), cum[:, :, CH - 1:CH].to_broadcast([P, KT * NCH, CH]),
                   cum, ALU.subtract).then_inc(sig("decay1"), 1)
                dve.wait_ge(sig("decay_exp1"), 1)
                step(tt(KK1, KK1, T1, ALU.mult))
                for k in range(KT):
                    ins = ts(T2[:, k, :], KK1[:, k, :], om[:, k:k + 1], ALU.mult)
                ins.then_inc(sig("kdec1"), 1)
                modulation()
                for t in range(2):
                    for g in range(2):
                        take(f"kdT1.{t}{g}", KTOK1[:, t, g * 512:(g + 1) * 512], lambda b: b[:, :])
                for c in range(NCH):
                    for g in range(2):
                        b = filled(dve, f"kv1.{c}{g}")
                        if c == 0:
                            ins = dve.tensor_copy(ST1[:, 4 * g:4 * g + 4, :], halves(b, P))
                        else:
                            for j in range(4):
                                h = 4 * g + j
                                ins = stt(ST1[:, 8 * c + h, :], ST1[:, 8 * (c - 1) + h, :],
                                          TOT1[:, h * NCH + c:h * NCH + c + 1], bank[b][:, j * P:(j + 1) * P],
                                          ALU.mult, ALU.add)
                        ins.then_inc(free[b], 1)
                    for g in range(2):
                        emptied(dve, f"kv1.{c}{g}")
                for g in range(4):
                    take(f"o1.{g}", T1[:, 2 * g:2 * g + 2, :])
                modulation()
                dve.wait_ge(sig("ostd1"), 1)
                step(tt(T1, T1, KK1, ALU.mult))
                emptied(dve, "g1.3")
                stt(H[:, :, 0:S], T1, column("hgrn_head_norm"), G1, ALU.mult, ALU.mult).then_inc(sig("y1_ready"), 1)
                modulation()
                add_output("mix1")

            def ple(l):
                norm(f"ple{l}", "ple_norm", 8 * l)
                modulation()
                for c in range(4):
                    emptied(dve, f"pg{l}.{c}")
                    b = filled(dve, f"pp{l}.{c}")
                    step(tt(GT[:, c, :], GT[:, c, :], bank[b][:, :], ALU.mult))
                    xs = XC[:, 2 * c:2 * c + 2, 0:S]
                    tt(xs, GT[:, c, :].rearrange("p (a b) -> p a b", b=S), xs, ALU.add).then_inc(x_ready, 1)

            def block2_dve():
                for t in range(2):
                    for g in range(2):
                        b = filled(dve, f"ctx{t}{g}")
                        dve.tensor_copy(XC[:, 4 * g:4 * g + 4, S + t * P:S + (t + 1) * P],
                                        halves(b, P)).then_inc(x_ready, 1)
                rstd("between")
                for k in range(KT):
                    xs = XC[:, k, 0:S]
                    stt(xs, xs, column("final_norm", k), RSTD[:, 0:S], ALU.mult, ALU.mult).then_inc(x_ready, 1)

                def mod_norm(name, gains, g0, part, streams):
                    n = S * streams
                    g = col[:, COL[gains] + g0:COL[gains] + g0 + 8].unsqueeze(2).to_broadcast([P, 8, 2])
                    l = g0 // 8
                    MOD = MODS[:, l]
                    emptied(dve, f"mod{6 * l + 5}")
                    step(stt(CA, MOD[:, 8 * part + 8:8 * part + 16, :], 1.0, g, ALU.add, ALU.mult))
                    rstd(name)
                    for k in range(KT):
                        for s in range(streams):
                            ins = stt(H[:, k, s * S:(s + 1) * S], XC[:, k, s * S:(s + 1) * S], CA[:, k, s:s + 1],
                                      RSTD[:, s * S:(s + 1) * S], ALU.mult, ALU.mult)
                        ins.then_inc(scaled, 1)

                def softmaxes(kind, scale, out_view, between=None):
                    units = UNITS[kind]
                    comps = 2 if kind == "diff" else 1
                    st = ST_O if kind == "mla" else ST_E

                    def stats(u):
                        o = 8 * (u % 4)
                        return st[:, o:o + 2], st[:, o + 2:o + 4], st[:, o + 4:o + 6]

                    def maxima(u):
                        h, s, qt = units[u]
                        neg = stats(u)[0]
                        k0, k1 = key_range(kind, s)
                        for c in range(comps):
                            b = filled(dve, f"{kind}.s{u}.{c}")
                            src = bank[b][:, 0:k1 - k0]
                            if kind == "na" and s == 0:
                                if u >= 4:
                                    filled(dve, f"{kind}.t{u - 4}")
                                dve.wait_ge(sig(f"nbt{h % 2}"), 64 * (h // 2 + 1))
                                pr = probs(kind, u)
                                stt(pr[:, 0:S], bank[b][:, 0:S], scale, NBT[:, 2 * (h % 2) + qt, :], ALU.mult, ALU.add)
                                ts(pr[:, S:], bank[b][:, S:], scale, ALU.mult).then_inc(free[b], 1)
                                emptied(dve, f"{kind}.s{u}.{c}")
                                src = pr
                            ins = dve.tensor_reduce(neg[:, c:c + 1], src, AX_X, ALU.max)
                        step(ins)
                        ts(neg[:, 0:comps], neg[:, 0:comps], -1.0 if kind == "na" and s == 0 else -scale,
                           ALU.mult).then_inc(mx_ready, 1)

                    def normalise(u):
                        h, s, qt = units[u]
                        _, sums, rec = stats(u)
                        k0, k1 = key_range(kind, s)
                        n = k1 - k0
                        if kind == "na" and s == 0:
                            dve.wait_ge(exp_done, 2 * h + qt + 1)
                        else:
                            emptied(dve, f"{kind}.s{u}.{comps - 1}")
                        step(dve.reciprocal(rec[:, 0:comps], sums[:, 0:comps]))
                        p0 = probs(kind, u)[:, 0:n]
                        if comps == 2:
                            p1 = probs(kind, u, 1)[:, 0:n]
                            step(ts(rec[:, 1:2], rec[:, 1:2], LAM[:, 2:3], ALU.mult))
                            step(ts(p1, p1, rec[:, 1:2], ALU.mult))
                            stt(p0, p0, rec[:, 0:1], p1, ALU.mult, ALU.add).then_inc(a_ready, 1)
                        else:
                            ts(p0, p0, rec[:, 0:1], ALU.mult).then_inc(a_ready, 1)

                    def output(pair):
                        h, s, _ = units[2 * pair]
                        b = filled(dve, f"{kind}.o{pair}")
                        o, rows_ = out_view(h, s)
                        dve.tensor_copy(o, bank[b][rows_[0]:rows_[1], 0:S]).then_inc(free[b], 1)

                    for u in range(len(units) + 4):
                        if u < len(units):
                            maxima(u)
                        if 1 <= u <= len(units):
                            normalise(u - 1)
                        if u >= 4 and u % 2 == 0 and (u - 4) // 2 < len(units) // 2:
                            output((u - 4) // 2)
                        if between is not None:
                            between(u)

                def gated_output(name, part, streams):
                    for f in range(KT):
                        if streams == 2:
                            b = filled(dve, f"{name}.out{f // 2}.{f % 2}")
                        else:
                            b = filled(dve, f"{name}.out{f // 2}")
                        for s in range(streams):
                            src = bank[b][:, s * S:(s + 1) * S] if streams == 2 else bank[b][:, (f % 2) * S:(f % 2 + 1) * S]
                            xs = XC[:, f, s * S:(s + 1) * S]
                            stt(xs, src, MODS[:, ("even", "odd").index(name), 8 * part + f, s:s + 1], xs, ALU.mult, ALU.add).then_inc(x_ready, 1)

                def even():
                    mod_norm("even", "norm_mix_2", 0, 0, 2)
                    dve.wait_ge(sig("lamrow_in"), 16)
                    lr = AT_E[:, 0, :].rearrange("p (a b n) -> p a b n", a=2, b=2)
                    prod = AT_E[:, 1, 0:P].rearrange("p (a n) -> p a n", a=2)
                    step(tt(prod, lr[:, :, 0, :], lr[:, :, 1, :], ALU.mult))
                    dve.tensor_reduce(LAM[:, 0:2], prod, AX_X, ALU.add).then_inc(sig("lam_sums"), 1)
                    for n in range(2):
                        for t in range(2):
                            take(f"kd{n}.{t}", KD[:, 2 * n + t, :], lambda b: b[:, :])
                    emptied(dve, "qd0.0"), emptied(dve, "qd0.1"), emptied(dve, "qd1.0"), emptied(dve, "qd1.1")
                    dve.wait_ge(sig("tb_e"), 16)
                    for name, src in (("rq", QD), ("rk", KD)):
                        for n in range(2):
                            b = filled(dve, f"{name}{n}")
                            tt(TMP[:, 2 * n:2 * n + 2, :], halves(b), SIN.unsqueeze(1).to_broadcast([P, 2, S]),
                               ALU.mult).then_inc(free[b], 1)
                        xs = src[:, :, 0:S]
                        step(tt(xs, xs, COS.unsqueeze(1).to_broadcast([P, 4, S]), ALU.mult))
                        emptied(dve, f"{name}1")
                        ins = tt(xs, xs, TMP, ALU.add)
                        ins.then_inc(sig("rope"), 1)
                        dve.wait_ge(sig("rope"), 1 if name == "rq" else 2)
                    for n in range(2):
                        for t in range(2):
                            take(f"kn{n}.{t}", KN[:, 2 * n + t, :], lambda b: b[:, :])
                    dve.wait_ge(sig("lam_exp"), 1)
                    step(tt(LAM[:, 2:3], LAM[:, 1:2], LAM[:, 0:1], ALU.subtract))
                    step(ts(LAM[:, 2:3], LAM[:, 2:3], -LAM_INIT, ALU.add))
                    softmaxes("diff", 64 ** -0.5, lambda h, s: (H[:, h, s * S:(s + 1) * S], (0, P)))

                    def head_norm(u):
                        h, late = (u - 14) // 2, u % 2
                        if 0 <= h < 4 and not late:
                            dve.wait_ge(sig("ystd"), h + 1)
                            ts(YRS[:, h, :], YRS[:, h, :], column("diff_subln_2"), ALU.mult, 1.0 - LAM_INIT,
                               ALU.mult).then_inc(sig("ygain"), 1)
                        if 0 <= h < 4 and late:
                            dve.wait_ge(sig("ygain"), h + 1)
                            tt(H[:, h, :], H[:, h, :], YRS[:, h, :], ALU.mult).then_inc(sig("ye_ready"), 1)

                    softmaxes("na", 64 ** -0.5, lambda h, s: (
                        H[64 * (h % 2):64 * (h % 2) + 64, 4 + h // 2, s * S:(s + 1) * S],
                        (64 * (h % 2), 64 * (h % 2) + 64)), head_norm)
                    gated_output("even", 2, 2)

                def odd():
                    mod_norm("odd", "norm_mix_2", 8, 0, 2)
                    dve.wait_ge(sig("logit_ln"), 1)
                    min0_minus(LOGG, LOGG, SD[:, 0, 0:8]).then_inc(sig("logg"), 1)
                    take("cq", CQ)
                    take("ckv", CKV, lambda b: b[:, :])
                    take("rk.0", RK[:, 0, :], lambda b: b[:, :])
                    take("rk.1", RK[:, 1, :], lambda b: b[:, :])
                    dve.wait_ge(sig("cstd"), 1)
                    for k in range(2):
                        ins = stt(CQ[:, k, :], CQ[:, k, :], column("mla_q_norm_2", k), CSQ[:, 0:S], ALU.mult, ALU.mult)
                    ins.then_inc(sig("latents"), 1)
                    stt(CKV, CKV, column("mla_kv_norm_2"), CSQ[:, 512:1024], ALU.mult, ALU.mult).then_inc(sig("latents"), 1)
                    dve.wait_ge(sig("tb_o"), 16)
                    emptied(dve, "kr")
                    b = filled(dve, "krr")
                    tt(CSQ[64:96, 0:S], bank[b][64:96, 0:S], SINM[64:96, :], ALU.mult).then_inc(free[b], 1)
                    step(tt(KR[64:96, 0:S], KR[64:96, 0:S], COSM[64:96, :], ALU.mult))
                    emptied(dve, "krr")
                    step(tt(KR[64:96, 0:S], KR[64:96, 0:S], CSQ[64:96, 0:S], ALU.add))
                    dve.tensor_copy(KM[64:96, :, :], KR[64:96, :].unsqueeze(1).to_broadcast([32, 8, 512])).then_inc(sig("rope_m"), 1)
                    for n in range(4):
                        emptied(dve, f"qm{n}")
                    for n in range(4):
                        b = filled(dve, f"qr{n}")
                        step(tt(QTMP[0:96, n % 2], halves(b)[0:96], SINM[0:96, :].unsqueeze(1).to_broadcast([96, 2, S]), ALU.mult))
                        qs = QM[0:96, 2 * n:2 * n + 2, :]
                        step(tt(qs, qs, COSM[0:96, :].unsqueeze(1).to_broadcast([96, 2, S]), ALU.mult))
                        tt(qs, qs, QTMP[0:96, n % 2], ALU.add).then_inc(free[b], 1)
                    emptied(dve, "qr3")
                    for h in range(0, 8, 2):
                        take(f"kn.{h}", KM[0:64, h, :], lambda b: b[0:64, :])
                    softmaxes("mla", 96 ** -0.5, lambda h, s: (
                        H[64 * (h % 2):64 * (h % 2) + 64, h // 2, 0:S], (64 * (h % 2), 64 * (h % 2) + 64)))
                    dve.wait_ge(sig("dist_in"), 32)
                    DF, DB = XC[:, 0:4, S:2 * S], XC[:, 4:8, S:2 * S]
                    for h in range(4):
                        lf, lb = LOGG[:, h:h + 1], LOGG[:, 4 + h:5 + h]
                        step(ts(DT[:, 0:2, :], DF[:, 0:2, :], lf, ALU.mult))
                        stt(DT[:, 0:2, :], DB[:, 0:2, :], lb, DT[:, 0:2, :], ALU.mult, ALU.add).then_inc(sig("dt_arg"), 1)
                        dve.wait_ge(sig("dt_exp"), h + 1)
                        step(tt(DT[:, 2:4, :], DT[:, 2:4, :], DT2, ALU.add))
                        if h:
                            filled(dve, f"ro{h - 1}")
                        for n in range(2):
                            b = filled(dve, f"rs{h}.{n}")
                            stt(SD[:, 2 * n:2 * n + 2, :], halves(b), 64 ** -0.5, DT[:, 2 * n:2 * n + 2, :],
                                ALU.mult, ALU.mult).then_inc(free[b], 1)
                        emptied(dve, f"rs{h}.1")
                        if h:
                            take(f"ro{h - 1}", RO[:, h - 1, :], lambda b: b[:, 0:S])
                    take("ro3", RO[:, 3, :], lambda b: b[:, 0:S])
                    dve.wait_ge(sig("rstd"), 1)
                    emptied(dve, "rg1")
                    step(tt(RO, RO, RORS, ALU.mult))
                    tt(H[:, 4:8, 0:S], RO, RG, ALU.mult).then_inc(sig("yo_ready"), 1)
                    gated_output("odd", 2, 1)

                def moe(l):
                    ns, slots, groups, nt = experts(l)
                    T2_ = 2 * ns
                    mod_norm(f"moe{l}", "norm_ffn_2", 8 * l, 3, ns)
                    take(f"rw{l}", LGT[0:NE, 0:nt], lambda b: b[0:NE, 0:nt])
                    b = filled(dve, f"rt{l}")
                    lg, mx = LG[:, 0:T2_, :], LMX[:, 0:T2_]
                    step(dve.tensor_copy(lg, bank[b][:, 0:T2_ * NE].rearrange("p (t e) -> p t e", e=NE)))
                    dve.tensor_reduce(mx, lg, AX_X, ALU.max).then_inc(free[b], 1)
                    emptied(dve, f"rt{l}")
                    tt(lg, lg, mx.unsqueeze(2).to_broadcast([P, T2_, NE]), ALU.subtract).then_inc(sig("lg_ready"), 1)
                    for t in range(T2_):
                        for g in range(2):
                            if (t + g) % 2:
                                take(f"tm{l}.{t}{g}", TM[:, t, g * 512:(g + 1) * 512], lambda b: b[:, :])
                    dve.wait_ge(sig("lg_exp"), l + 1)
                    step(dve.tensor_reduce(mx, lg, AX_X, ALU.add))
                    step(dve.reciprocal(mx, mx))
                    tt(AF[:, 0:T2_, :], lg, mx.unsqueeze(2).to_broadcast([P, T2_, NE]), ALU.mult).then_inc(sig("aff_ready"), 1)
                    take(f"aft{l}", AFT[0:NE, 0:nt], lambda b: b[0:NE, 0:nt])
                    emptied(dve, f"aft{l}")
                    for s in range(ns):
                        w = AFT[0:NE, s * S:(s + 1) * S]
                        for r in range(0, CAP, 8):
                            step(dve.max(TV[0:NE, s, r:r + 8], w))
                            step(dve.max_index(TI[0:NE, s, r:r + 8].bitcast(U32), TV[0:NE, s, r:r + 8], w))
                            step(dve.match_replace(w, TV[0:NE, s, r:r + 8], w, -1.0))
                    step(dve.tensor_copy(TIF[0:NE, 0:ns, :], TI[0:NE, 0:ns, :].bitcast(U32)))
                    tif, tv = [v[0:NE, 0:ns, :].rearrange("p s c -> p (s c)").unsqueeze(1) for v in (TIF, TV)]
                    tt(BD[0:NE, 0:NE * slots].rearrange("p (e c) -> p e c", c=slots), tif.to_broadcast([NE, NE, slots]),
                       ident[0:NE, 0:NE].unsqueeze(2).to_broadcast([NE, NE, slots]), ALU.mult)
                    ins = dve.tensor_copy(GREP[0:NE, :].rearrange("p (g c) -> p g c", c=slots),
                                          tv.to_broadcast([NE, groups, slots]))
                    step(ins)
                    if ns == 2:
                        step(ts(TIF[0:NE, 1, :], TIF[0:NE, 1, :], float(S), ALU.add))
                    dve.tensor_copy(IREP[0:NE, :].rearrange("p (g c) -> p g c", c=slots),
                                    tif.to_broadcast([NE, groups, slots])).then_inc(sig("top_ready"), 1)
                    per = 512 // slots
                    for n in range(ns):
                        b = filled(dve, f"ib{l}.{n}")
                        v = bank[b][:, :].rearrange("p (e c) -> p e c", c=slots)
                        for t in range(T2_):
                            s = t // 2
                            ins = ts(PM[:, t, n * per * CAP:(n + 1) * per * CAP].rearrange("p (e c) -> p e c", c=CAP),
                                     v[:, :, s * CAP:(s + 1) * CAP], const("iota_p")[:, t:t + 1], ALU.is_equal)
                        ins.then_inc(free[b], 1)
                        emptied(dve, f"ib{l}.{n}")
                    b = filled(dve, f"ic{l}")
                    dve.tensor_copy(IC, bank[b][:, 0:NE])
                    dve.tensor_copy(GC, bank[b][:, NE:2 * NE]).then_inc(free[b], 1)
                    emptied(dve, f"ic{l}")
                    for s in range(ns):
                        for k in range(1, KT, 2):
                            take(f"xe{l}.{s}{k}", xe_view(l, s, k), lambda b: b[:, :].rearrange("p (e c) -> p e c", c=CAP))
                    filled(dve, f"xe{l}.{ns - 1}7")
                    dve.wait_ge(sig("iof_in"), 16 * l + 16)
                    for s in range(ns):
                        for k in range(0, KT, 2):
                            emptied(dve, f"xe{l}.{s}{k}")
                    emptied(dve, f"xe{l}.{ns - 1}7")
                    xe = XE[:, 0:KT, :] if ns == 2 else XE1

                    def gather(e, i):
                        dve.tensor_copy(XCUR[:, 0:KT * slots].rearrange("p (k c) -> p k c", c=slots),
                                        xe[:, :, bass.ds(e * slots, slots)]).then_inc(xcur_ready, 1)

                    def one_hot(e):
                        dve.tensor_scalar(PG[:, 0:nt], IOF[:, 0:nt], IC[:, bass.ds(e, 1)], GC[:, bass.ds(e, 1)],
                                          ALU.is_equal, ALU.mult).then_inc(pg_ready, 1)

                    def expert(pre, i):
                        for half in range(2):
                            b = filled(dve, f"{pre}h3{'ab'[half]}", i)
                            dve.tensor_copy(P3[:, half * 512:(half + 1) * 512], bank[b][:, :]).then_inc(free[b], 1)
                        emptied(dve, f"{pre}s1", i)
                        b = filled(dve, f"{pre}s3", i)
                        tt(HIDT[:, 0:KT * slots], SILT[:, 0:KT * slots], bank[b][:, 0:KT * slots], ALU.mult).then_inc(free[b], 1)

                    def accumulate(pre, i, count):
                        dve.wait_ge(pg_ready, count)
                        for k in range(KT):
                            b = filled(dve, f"{pre}f{k}", i)
                            tt(MACC[:, k, 0:nt], MACC[:, k, 0:nt], bank[b][:, 0:nt], ALU.add).then_inc(free[b], 1)

                    gather(0, None)
                    expert(f"m{l}.p.", None)
                    step(dve.memset(MACC[:, :, 0:nt], 0.0))
                    one_hot(0)
                    with dve.Fori(0, NE - 1) as i:
                        gather(i + 1, i)
                        expert(f"m{l}.", i)
                        accumulate(f"m{l}.", i, NE * l + 1 + i)
                        one_hot(i + 1)
                    accumulate(f"m{l}.z.", None, NE * l + NE)
                    emptied(dve, f"m{l}.z.f7")
                    for k in range(KT):
                        for s in range(ns):
                            xs = XC[:, k, s * S:(s + 1) * S]
                            stt(xs, MACC[:, k, s * S:(s + 1) * S], MODS[:, l, 40 + k, s:s + 1], xs,
                                ALU.mult, ALU.add).then_inc(x_ready, 1)

                even()
                moe(0)
                odd()
                moe(1)
                norm("final", "final_norm_2", 0)
                for t in range(2):
                    for g in range(2):
                        take(f"out{t}{g}", OUTT[:, t, g * 512:(g + 1) * 512], lambda b: b[:, :])

            feed_forward(0)
            mixer0()
            feed_forward(1)
            ple(0)
            feed_forward(2)
            mixer1()
            feed_forward(3)
            ple(1)
            block2_dve()

        @block.scalar
        def _(act):
            steps = [0]

            def f(o, i, func, **kw):
                return act.activation(o, i, func, **kw)

            def step(ins):
                steps[0] += 1
                ins.then_inc(act_step, 1)
                act.wait_ge(act_step, steps[0])

            def take(name, o, func=ACT.Copy, view=None, **kw):
                b = filled(act, name)
                v = halves(b) if view is None else view(bank[b])
                f(o, v, func, **kw).then_inc(free[b], 1)

            parts = [0]

            def modulation():
                n = parts[0]
                parts[0] += 1
                if n < 12:
                    take(f"ada{n}a", APART[:, 0:2, :])

            def log_mean(name, o, width, n=512):
                b = filled(act, name)
                f(o, bank[b][:, 0:n], ACT.Ln, bias=const("eps"), scale=1.0 / width).then_inc(free[b], 1)

            def norm_squares(name, after, n=S):
                count = dict(X_WRITES)[after]
                for k in range(KT):
                    if after == "between":
                        act.wait_ge(x_ready, X_AT[after] - KT + k + 1)
                    elif after != "init":
                        act.wait_ge(x_ready, X_AT[after] - count + -(-(k + 1) * count // KT))
                    elif k == 0:
                        act.wait_ge(x_ready, X_AT[after])
                    f(SQ[:, k, 0:n], XC[:, k, 0:n], ACT.Square).then_inc(sq_ready, 1)
                log_mean(f"norm.{name}", STD[:, 0:n], D, n)
                emptied(act, f"norm.{name}")
                f(RSTD[:, 0:n], STD[:, 0:n], ACT.Exp, scale=-0.5).then_inc(std_ready, 1)

            def add_shift(l, part, streams, base):
                emptied(act, f"mod{6 * l + 5}")
                for k in range(KT):
                    act.wait_ge(scaled, base + k + 1)
                    for s in range(streams):
                        hs = H[:, k, s * S:(s + 1) * S]
                        f(hs, hs, ACT.Identity, bias=MODS[:, l, 8 * part + k, s:s + 1]).then_inc(h_ready, 1)

            def feed_forward(k, after):
                norm_squares(f"ffn{k}", after)
                if k:
                    modulation()

                def silu(s, i=0, first=False):
                    act.wait_ge(up_full, 2 * (FSTEPS * k + s) + 1 + 8 * i)
                    if not first:
                        act.wait_ge(hid_ready, FSTEPS * k + s - 1 + 4 * i)
                    f(SIL[s % 2], bank[4 + 2 * (s % 2)][:, :], ACT.Silu).then_inc(silu_done, 1)

                silu(0, first=True)
                silu(1, first=True)
                with act.Fori(0, 2) as i:
                    for j in range(4):
                        silu(2 + j, i)
                silu(FSTEPS - 1)

            act.dma_start(cst[:, :], T["const"]).then_inc(cst_in, 16)
            for n, (vecs, _, _) in enumerate(VEC_GROUPS):
                row = 0
                for name, rows in vecs:
                    act.dma_start(ROWS_IN[row:row + rows, n, :], T[name]).then_inc(vec_in, 16)
                    row += rows

            act.wait_ge(sig("sc_raw"), 1)
            f(SC[:, :, 0:2], SC[:, :, 0:2], ACT.Silu).then_inc(sig("sc_ready"), 1)

            def mixer0():
                lam = col[:, COL["lru_lambda"]:COL["lru_lambda"] + 4]
                act.wait_ge(x_ready, X_AT["ffn0"])
                step(f(LC[:, 8:12], lam, ACT.Abs))
                step(f(LC[:, 8:12], LC[:, 8:12], ACT.Exp, scale=-1.0))
                f(LC[:, 8:12], LC[:, 8:12], ACT.Ln, bias=1.0).then_inc(sig("lam_ln"), 1)
                norm_squares("mix0", "ffn0")
                modulation()
                take("q0", Q0, scale=float(64) ** -0.5)
                take("v0a", V0[:, :, 0:S])
                take("v0b", V0[:, :, S:])
                emptied(act, "gate")
                step(f(L0, Z0, ACT.Abs))
                step(f(L0, L0, ACT.Exp, scale=-1.0))
                f(L0, L0, ACT.Ln, bias=1.0).then_inc(sig("gate_ln"), 1)
                take("g0a", G0[:, 0:2, :], ACT.Silu)
                take("g0b", G0[:, 2:4, :], ACT.Silu)
                take("xg0", XG[:, 0:2, :], ACT.Gelu_apprx_tanh)
                take("xg1", XG[:, 2:4, :], ACT.Gelu_apprx_tanh)
                modulation()
                act.wait_ge(sig("decay0"), 1)
                f(TOT0, flat(CUM0).rearrange("p (c t) -> p c t", t=CH)[:, :, CH - 1], ACT.Exp)
                f(L0, L0, ACT.Exp).then_inc(sig("decay_exp0"), 1)
                for n in range(4):
                    b = filled(act, f"lru{n}")
                    for j in range(2):
                        i = 2 * (n % 2) + j
                        ins = f((RA, IX)[n // 2][:, i, :], bank[b][:, j * S:(j + 1) * S], ACT.Sigmoid,
                                bias=column(("lru_ba", "lru_bx")[n // 2], i))
                    ins.then_inc(free[b], 1)
                act.wait_ge(sig("lam_ready"), 1)
                emptied(act, "lru1")
                for i in range(4):
                    f(AA[:, i, :], RA[:, i, :], ACT.Exp, scale=LC[:, i:i + 1])
                for i in range(4):
                    ins = f(TH[:, i, :], RA[:, i, :], ACT.Tanh, scale=LC[:, 4 + i:5 + i])
                ins.then_inc(sig("lru_exp"), 1)
                emptied(act, "o0.0")
                emptied(act, "o0.1")
                f(OSQ0, O0, ACT.Square).then_inc(sig("osq0"), 1)
                modulation()
                for n in range(2):
                    log_mean(f"on0.{n}", flat(ORS0)[:, n * 512:(n + 1) * 512], P)
                emptied(act, "on0.0")
                emptied(act, "on0.1")
                f(ORS0, ORS0, ACT.Exp, scale=-0.5).then_inc(sig("ostd0"), 1)
                act.wait_ge(sig("lru_arg"), 1)
                f(U0, U0, ACT.Sqrt).then_inc(sig("lru_root"), 1)
                modulation()

            def mixer1():
                norm_squares("mix1", "ffn2")
                modulation()
                _, e0, e1, lb, om, ln_lb, ln_om, _, _ = [LB[:, n, :] for n in range(9)]
                act.wait_ge(sig("lb_arg"), 1)
                f(e0, e0, ACT.Exp)
                f(e1, e1, ACT.Exp).then_inc(sig("lb_exp"), 1)
                act.wait_ge(sig("lb_ready"), 1)
                f(ln_lb, lb, ACT.Ln)
                f(ln_om, om, ACT.Ln)
                for c in range(4):
                    emptied(act, f"z1.{c}")
                step(f(T1, Z1, ACT.Abs))
                step(f(T1, T1, ACT.Exp, scale=-1.0))
                f(T1, T1, ACT.Ln, bias=1.0).then_inc(sig("ln1a"), 1)
                for c in range(4):
                    take(f"v1.{c}", V1[:, :, c * S:(c + 1) * S])
                act.wait_ge(sig("ls1"), 1)
                for k in range(KT):
                    ins = f(T2[:, k, :], T1[:, k, :], ACT.Abs, bias=LB[:, 7, k:k + 1])
                step(ins)
                step(f(T2, T2, ACT.Exp, scale=-1.0))
                f(T2, T2, ACT.Ln, bias=1.0).then_inc(sig("ln1b"), 1)
                f(KK1, Z1, ACT.Sigmoid, scale=-1.0)
                for c in range(4):
                    take(f"q1.{c}", Q1[:, 2 * c:2 * c + 2, :], ACT.Silu)
                act.wait_ge(sig("decay1"), 1)
                f(TOT1, flat(T2).rearrange("p (c t) -> p c t", t=CH)[:, :, CH - 1], ACT.Exp)
                f(T1, T1, ACT.Exp).then_inc(sig("decay_exp1"), 1)
                for c in range(4):
                    take(f"g1.{c}", G1[:, 2 * c:2 * c + 2, :], ACT.Silu)
                modulation()
                for g in range(4):
                    emptied(act, f"o1.{g}")
                f(T2, T1, ACT.Square).then_inc(sig("osq1"), 1)
                modulation()
                for g in range(4):
                    log_mean(f"on1.{g}", flat(KK1)[:, g * 512:(g + 1) * 512], P)
                for g in range(4):
                    emptied(act, f"on1.{g}")
                f(KK1, KK1, ACT.Exp, scale=-0.5).then_inc(sig("ostd1"), 1)
                modulation()

            def ple(l, after):
                norm_squares(f"ple{l}", after)
                modulation()
                for c in range(4):
                    take(f"pg{l}.{c}", GT[:, c, :], ACT.Sigmoid, lambda b: b[:, :])

            def block2_act():
                act.dma_start(CTXIN, T["ctx_2"].rearrange("(t p) f -> p t f", p=P)).then_inc(ctx_in, 16)
                norm_squares("between", "ple1")
                act.dma_start(LOGG, T["ret_decay_logit_2"].to_broadcast([P, 8])).then_inc(sig("logit_in"), 16)
                for n in range(8):
                    take(f"hot{n}", NB[0:56, n * 512:(n + 1) * 512], view=lambda b: b[0:56, :])

                LAG = 2

                def softmaxes(kind, scale, between=None):
                    units = UNITS[kind]
                    comps = 2 if kind == "diff" else 1
                    st = ST_O if kind == "mla" else ST_E

                    def exps(u):
                        h, s, qt = units[u]
                        o = 8 * (u % 4)
                        neg, sums = st[:, o:o + 2], st[:, o + 2:o + 4]
                        k0, k1 = key_range(kind, s)
                        n = k1 - k0
                        act.wait_ge(mx_ready, UNITS_BEFORE[kind] + u + 1)
                        if u >= DEPTH[kind]:
                            filled(act, f"{kind}.t{u - DEPTH[kind]}")
                        for c in range(comps):
                            pr = probs(kind, u, c)[:, 0:n]
                            if kind == "na" and s == 0:
                                f(pr, pr, ACT.Exp, bias=neg[:, c:c + 1], accum_out=sums[:, c:c + 1]).then_inc(exp_done, 1)
                            else:
                                b, _, _, _ = tiles[f"{kind}.s{u}.{c}"]
                                f(pr, bank[b][:, 0:n], ACT.Exp, bias=neg[:, c:c + 1], scale=scale,
                                  accum_out=sums[:, c:c + 1]).then_inc(free[b], 1)

                    def turned(u):
                        _, s, qt = units[u]
                        n = 4 if s == 0 else 2
                        b = filled(act, f"{kind}.t{u}")
                        f(probs_T(kind, u // 2)[:, 0:n, qt * P:(qt + 1) * P],
                          bank[b][:, 0:n * P].rearrange("p (k q) -> p k q", q=P), ACT.Copy).then_inc(free[b], 1)

                    for u in range(len(units) + LAG):
                        if u < len(units):
                            exps(u)
                        if u >= LAG:
                            turned(u - LAG)
                        if between is not None:
                            between(u)

                def even():
                    norm_squares("even", "between", 2 * S)
                    act.wait_ge(nb_in, 16)
                    act.dma_start(AT_E[:, 0, :], T["diff_lambda_2"].to_broadcast([P, 256])).then_inc(sig("lamrow_in"), 16)
                    o, w = LATE["rot_d"][0], 640
                    act.dma_start(TB_E, T["late"][:, o:o + w]).then_inc(sig("tb_e"), 16)
                    add_shift(0, 0, 2, 0)
                    for n in range(2):
                        for t in range(2):
                            take(f"qd{n}.{t}", QD[:, 2 * n + t, :], view=lambda b: b[:, :])
                    act.wait_ge(sig("lam_sums"), 1)
                    f(LAM[:, 0:2], LAM[:, 0:2], ACT.Exp).then_inc(sig("lam_exp"), 1)
                    for n in range(2):
                        for t in range(2):
                            take(f"vd{n}.{t}", VD[:, 2 * t:2 * t + 2, n * S:(n + 1) * S])
                    for n in range(2):
                        for t in range(2):
                            take(f"qn{n}.{t}", QN[:, 2 * n + t, :], view=lambda b: b[:, :])
                    for n in range(2):
                        for t in range(2):
                            take(f"vn{n}.{t}", VN[:, 2 * t:2 * t + 2, n * S:(n + 1) * S])
                    softmaxes("diff", 64 ** -0.5)

                    def head_norm(u):
                        h = u - 4
                        if 0 <= h < 4:
                            if h == 0:
                                for pair in range(8):
                                    emptied(act, f"diff.o{pair}")
                            f(YSQ[:, h, :], H[:, h, :], ACT.Square).then_inc(sig("ysq"), 1)
                        h, late = (u - 12) // 2, u % 2
                        if 0 <= h < 4 and not late:
                            log_mean(f"yn{h}", YRS[:, h, :], P)
                        if 0 <= h < 4 and late:
                            emptied(act, f"yn{h}")
                            f(YRS[:, h, :], YRS[:, h, :], ACT.Exp, scale=-0.5).then_inc(sig("ystd"), 1)

                    softmaxes("na", 64 ** -0.5, head_norm)

                def odd():
                    act.wait_ge(x_ready, X_AT["moe0"])
                    o, w = LATE["rot_m"][0], 640
                    act.dma_start(TB_O, T["late"][:, o:o + w]).then_inc(sig("tb_o"), 16)
                    norm_squares("odd", "moe0", 2 * S)
                    add_shift(1, 0, 2, 16)
                    act.wait_ge(sig("logit_in"), 16)
                    lt = SD[:, 0, 0:8]
                    step(f(lt, LOGG, ACT.Abs))
                    step(f(lt, lt, ACT.Exp, scale=-1.0))
                    f(lt, lt, ACT.Ln, bias=1.0).then_inc(sig("logit_ln"), 1)
                    act.wait_ge(h_ready, H_AT["odd"])
                    for n, name in enumerate(("dist_f", "dist_b")):
                        o, w = LATE[name]
                        act.dma_start(XC[:, 4 * n:4 * n + 4, S:2 * S],
                                      T["late"][:, o:o + w].rearrange("p (a b) -> p a b", b=S)).then_inc(sig("dist_in"), 16)
                    take("kr", KR[64:96, :], view=lambda b: b[64:96, :])
                    take("rq", RQ)
                    emptied(act, "cq")
                    f(CSQ[:, 0:512], flat(CQ), ACT.Square).then_inc(sig("csq"), 1)
                    emptied(act, "ckv")
                    f(CSQ[:, 512:1024], CKV, ACT.Square).then_inc(sig("csq"), 1)
                    for t in range(2):
                        take(f"rv0.{t}", RV[:, 2 * t:2 * t + 2, 0:S])
                    log_mean("cqn", CSQ[:, 0:S], 256, S)
                    log_mean("ckvn", CSQ[:, 512:1024], P)
                    emptied(act, "cqn")
                    f(CSQ[:, 0:S], CSQ[:, 0:S], ACT.Exp, scale=-0.5)
                    emptied(act, "ckvn")
                    f(CSQ[:, 512:1024], CSQ[:, 512:1024], ACT.Exp, scale=-0.5).then_inc(sig("cstd"), 1)
                    for t in range(2):
                        take(f"rv1.{t}", RV[:, 2 * t:2 * t + 2, S:2 * S])
                    for n in range(2):
                        take(f"rg{n}", RG[:, 2 * n:2 * n + 2, :], ACT.Silu)
                    for n in range(4):
                        take(f"qm{n}", QM[0:96, 2 * n:2 * n + 2, :], view=lambda b: b[0:96, :].rearrange("p (a b) -> p a b", b=S))
                    for h in range(1, 8, 2):
                        take(f"kn.{h}", KM[0:64, h, :], view=lambda b: b[0:64, :])
                    for t in range(4):
                        take(f"vm{t}", VM[:, t, :], view=lambda b: b[:, :])
                    softmaxes("mla", 96 ** -0.5)
                    act.wait_ge(sig("dist_in"), 32)
                    for h in range(4):
                        act.wait_ge(sig("dt_arg"), h + 1)
                        f(DT[:, 0:2, :], DT[:, 0:2, :], ACT.Exp)
                        f(DT[:, 2:4, :], XC[:, 2:4, S:2 * S], ACT.Exp, scale=LOGG[:, h:h + 1])
                        f(DT2, XC[:, 6:8, S:2 * S], ACT.Exp, scale=LOGG[:, 4 + h:5 + h]).then_inc(sig("dt_exp"), 1)
                    emptied(act, "ro3")
                    f(ROSQ, RO, ACT.Square).then_inc(sig("rosq"), 1)
                    for n in range(2):
                        log_mean(f"rn{n}", flat(RORS)[:, n * 512:(n + 1) * 512], P)
                    emptied(act, "rn0")
                    emptied(act, "rn1")
                    f(RORS, RORS, ACT.Exp, scale=-0.5).then_inc(sig("rstd"), 1)

                def moe(l):
                    ns, slots, groups, nt = experts(l)
                    norm_squares(f"moe{l}", ("even", "odd")[l], nt)
                    add_shift(l, 3, ns, 16 * l + 8)
                    act.wait_ge(sig("lg_ready"), l + 1)
                    f(LG[:, 0:2 * ns, :], LG[:, 0:2 * ns, :], ACT.Exp).then_inc(sig("lg_exp"), 1)
                    for t in range(2 * ns):
                        for g in range(2):
                            if (t + g) % 2 == 0:
                                take(f"tm{l}.{t}{g}", TM[:, t, g * 512:(g + 1) * 512], view=lambda b: b[:, :])
                    for s in range(ns):
                        for k in range(0, KT, 2):
                            take(f"xe{l}.{s}{k}", xe_view(l, s, k),
                                 view=lambda b: b[:, :].rearrange("p (e c) -> p e c", c=CAP))

                    def expert(pre, i):
                        for half in range(2):
                            b = filled(act, f"{pre}h1{'ab'[half]}", i)
                            f(P1[:, half * 512:(half + 1) * 512], bank[b][:, :], ACT.Copy).then_inc(free[b], 1)
                        b = filled(act, f"{pre}s1", i)
                        f(SILT[:, 0:KT * slots], bank[b][:, 0:KT * slots], ACT.Silu).then_inc(free[b], 1)
                        for half in range(2):
                            b = filled(act, f"{pre}y{'ab'[half]}", i)
                            f(YS[:, half * 512:(half + 1) * 512], bank[b][:, :], ACT.Copy).then_inc(free[b], 1)

                    expert(f"m{l}.p.", None)
                    with act.Fori(0, NE - 1) as i:
                        expert(f"m{l}.", i)

                even()
                moe(0)
                odd()
                moe(1)
                norm_squares("final", "moe1")

            feed_forward(0, "init")
            mixer0()
            feed_forward(1, "mix0")
            ple(0, "ffn1")
            feed_forward(2, "ple0")
            mixer1()
            feed_forward(3, "mix1")
            ple(1, "ffn3")
            block2_act()

        @block.gpsimd
        def _(pool):
            def block2_pool():
                pool.wait_ge(x_ready, X_AT["mix1"])
                pool.memset(RPBT, 1.0).then_inc(pool_step, 1)
                pool.wait_ge(pool_step, 2)
                for h in range(8):
                    pool.dma_start(RPBT[0:31, 7 * h:7 * h + 7], T["na_rpb_2"][h, 4:11, :].rearrange("r j -> j r"),
                                   allow_slow_non_contiguous=True).then_inc(hot_in, 16)
                pool.dma_start(HOT[0:32, :], T["hot"]).then_inc(hot_in, 16)
                for n in range(8):
                    emptied(pool, f"hot{n}")
                pool.dma_start(nb_dram.rearrange("h r a b -> (h r) (a b)"), NB[0:56, :]).then_inc(nb_in, 16)
                pool.wait_ge(nb_in, 16)
                for h in range(8):
                    if h >= 2:
                        pool.wait_ge(mx_ready, UNITS_BEFORE["na"] + 4 * (h - 2) + 4)
                    for r in range(ROWS):
                        pool.dma_start(NBT[64 * (r % 2):64 * (r % 2) + 64, 2 * (h % 2) + r // 2, :].rearrange("p (a b) -> p a b", b=GRID),
                                       nb_dram[h, 3 - r:7 - r].rearrange("a c b -> c a b")).then_inc(sig(f"nbt{h % 2}"), 16)
                pool.wait_ge(x_ready, X_AT["even"])
                o, w = LATE["iota_f"]
                pool.dma_start(IOF, T["late"][:, o:o + w]).then_inc(sig("iof_in"), 16)
                pool.wait_ge(x_ready, X_AT["odd"])
                pool.dma_start(IOF, T["late"][:, o:o + w]).then_inc(sig("iof_in"), 16)

            pool.memset(WBD, 0.0).then_inc(pool_step, 1)
            pool.wait_ge(pool_step, 1)
            pool.dma_start(GUP[0:16, :], T["gla_gate_up"]).then_inc(small_in, 16)
            for n, name in enumerate(("lru_wa", "lru_wx")):
                for r in range(2):
                    pool.dma_start(WBD[64 * r:64 * r + 64, 4 * n:4 * n + 4, 64 * r:64 * r + 64],
                                   T[name].rearrange("(j r) i o -> r i j o", r=2)[r]).then_inc(small_in, 16)
            block2_pool()

        @block.sync
        def _(sp):
            loads = Ring()

            def load(src, *dims):
                s, n = loads.next()
                if loads.i is not None or n > 0:
                    sp.wait_ge(w_used[s], n)
                v = ring[:, s, 0:int(np.prod(dims))].rearrange("p (a b) -> p a b", b=dims[1])
                sp.dma_start(v, src).then_inc(w_in[s], 16)

            def rows(w):
                return w.rearrange("(k p) n -> p k n", p=P)

            def columns_of(w, at, n=256):
                load(rows(w)[:, :, at:at + n], w.shape[0] // P, n)

            parts = [0]

            def modulation():
                n = parts[0]
                parts[0] += 1
                if n < 12:
                    w, at = rows(T["ada_w_2"][n // 6]), n % 6 * D
                    for g in range(4):
                        load(w[:, 2 * g:2 * g + 2, at:at + D], 2, D)

            def feed_forward(f):
                if f:
                    modulation()
                w1, w3, w2 = [rows(T[name][f // 2, f % 2]) for name in ("ffn_w1", "ffn_w3", "ffn_w2")]

                def up(s):
                    for w in (w1, w3):
                        load(w[:, :, bass.ds(s * 256, 256)], KT, 256)

                def down(s):
                    load(w2[:, bass.ds(s * 2, 2), :], 2, D)

                up(0)
                up(1)
                down(0)
                if f == 0:
                    for s in range(2, FSTEPS - 1):
                        up(s)
                        down(s - 1)
                else:
                    with sp.Fori(0, 2) as i:
                        loads.loop(i)
                        for j in range(4):
                            up(4 * i + 2 + j)
                            down(4 * i + 1 + j)
                    loads.end(2)
                up(FSTEPS - 1)
                down(FSTEPS - 2)
                down(FSTEPS - 1)

            sp.dma_start(XIN, T["x"].rearrange("(t p) f -> p t f", p=P)).then_inc(x_in, 16)
            for l in range(2):
                sp.dma_start(PIN[:, 2 * l:2 * l + 2, :], T["p"][l].rearrange("(t p) f -> p t f", p=P)).then_inc(x_in, 16)

            def ple(l):
                modulation()
                for c in range(4):
                    columns_of(T["ple_gate"][l], c * 256)
                load(rows(T["ple_proj"][l]), 2, D)

            def output(w):
                for c in range(4):
                    columns_of(w, c * 256)

            def block2_sp():
                def moe(l):
                    load(rows(T["moe_router_2"][l]), KT, NE)

                    def expert(e):
                        for name in ("moe_w1_2", "moe_w3_2", "moe_w2_2"):
                            w = T[name][l].rearrange("e (q k p) n -> e q p k n", p=P, k=2)
                            for q in range(4):
                                if isinstance(e, int):
                                    load(w[e, q], 2, D)
                                else:
                                    load(w[bass.ds(e, 1), q].rearrange("a p k n -> (a p) k n"), 2, D)

                    expert(0)
                    with sp.Fori(0, NE - 1) as i:
                        loads.loop(i)
                        expert(i + 1)
                    loads.end(NE - 1)

                for at in (0, 256, 512, 768, 1024, 1280, 1536, 1792, 2048, 2304, 2560, 2816):
                    columns_of(T["even_w_in_2"], at)
                output(T["even_w_out_2"])
                moe(0)
                w = T["odd_w_in_2"]
                for at, n in ((0, 256), (256, 160), (416, 256), (672, 256), (928, 256), (1184, 256),
                              (1440, 256), (1696, 256)):
                    columns_of(w, at, n)
                load(rows(T["mla_w_uq_2"]), 2, 768)
                load(rows(T["mla_w_ukv_2"]), 1, D)
                output(T["odd_w_out_2"])
                moe(1)
                for t in range(2):
                    for g in range(2):
                        emptied(sp, f"out{t}{g}")
                sp.dma_start(out.rearrange("(t p) f -> p t f", p=P), OUTT).then_inc(out_done, 16)
                sp.wait_ge(out_done, 16)

            sp.wait_ge(vec_in, 16 * sum(len(v) for v, _, _ in VEC_GROUPS))
            sp.wait_ge(x_in, 48)
            feed_forward(0)
            modulation()
            w = T["m0_w_in"]
            for at, n in ((1536, 16), (256, 256), (0, 256), (512, 256), (768, 256), (1552, 256), (1808, 256),
                          (1024, 256), (1280, 256), (2064, 256), (2320, 256)):
                columns_of(w, at, n)
            for _ in range(3):
                modulation()
            output(T["m0_w_out"])
            feed_forward(1)
            ple(0)
            feed_forward(2)
            modulation()
            for at in (1024, 2048, 0, 3072):
                for c in range(4):
                    columns_of(T["m1_w_in"], at + c * 256)
            for _ in range(3):
                modulation()
            output(T["m1_w_out"])
            feed_forward(3)
            ple(1)
            block2_sp()


SHAPES = {
    "x": (S, D), "p": (2, S, 256), "ffn_w1": (2, 2, D, FF), "ffn_w3": (2, 2, D, FF), "ffn_w2": (2, 2, FF, D),
    "ple_proj": (2, 256, D), "ple_gate": (2, D, D), "m0_w_in": (D, 2576), "gla_gate_up": (16, 256),
    "lru_wa": (8, 64, 64), "lru_wx": (8, 64, 64), "m0_w_out": (D, D), "m1_w_in": (D, 4096), "m1_w_out": (D, D),
    "ctx_2": (S, D), "ada_w_2": (2, D, 6 * D), "even_w_in_2": (D, 3 * D), "even_w_out_2": (D, D),
    "diff_lambda_2": (1, 256), "na_rpb_2": (8, 15, 31), "odd_w_in_2": (D, 1952), "odd_w_out_2": (D, D),
    "mla_w_uq_2": (256, 768), "mla_w_ukv_2": (P, D), "ret_decay_logit_2": (1, 8), "moe_router_2": (2, D, NE),
    "moe_w1_2": (2, NE, D, D), "moe_w3_2": (2, NE, D, D), "moe_w2_2": (2, NE, D, D),
}
for _vecs, _, _ in VEC_GROUPS:
    for _name, _rows in _vecs:
        SHAPES[_name] = (_rows, P)


def kernel(**inputs):
    import concourse.bacc as bacc
    from concourse.bass_utils import run_bass_kernel_spmd

    nc = bacc.Bacc("TRN2", target_bir_lowering=False, num_devices=1)
    resident, late, hot = constant_tables()
    arrays = {name: np.ascontiguousarray(inputs[name]).reshape(shape) for name, shape in SHAPES.items()}
    arrays.update(const=resident, late=late, hot=hot)
    T = {name: nc.dram_tensor(name, a.shape, mybir.dt.from_np(a.dtype), kind="ExternalInput").ap()
         for name, a in arrays.items()}
    out = nc.dram_tensor("out", (S, D), F32, kind="ExternalOutput").ap()
    two_blocks(nc, T, out)
    result = run_bass_kernel_spmd(nc, [arrays], core_ids=[0])
    return result.results[0]["out"].reshape(1, S, D)
```
